# Optimizing a Trainium2 kernel written in Bass

```python
import jax, jax.numpy as jnp
from jax import lax
import numpy as np

D_MODEL = 1024
BATCH = 1
SEQ = 512
DEPTH = 2

HEAD_DIM = 64
A_HEADS = 8
A_Q_RANK = 256
A_KV_RANK = 128
A_NOPE_DIM = 64
A_ROPE_DIM = 32
A_V_DIM = 64
B_HEADS = 8
B_BRANCHES = ((128, 1), (512, 4), (2048, 16))
C_HEADS = 16
GRID_W = 64
NA_ROWS = 8
NA_COLS = 16
NA_COL_BLOCK = 16
NA_BAND = NA_COL_BLOCK + NA_COLS
D_FF = -(-8 * D_MODEL // (3 * 256)) * 256

ROPE_THETA = 10000.0
EPS = 1e-6
Q_BLOCK = 128
NEG_INF = -1e30
N_EVEN = (DEPTH + 1) // 2
N_ODD = DEPTH // 2
EVEN_IN_COLS = A_Q_RANK + A_KV_RANK + A_ROPE_DIM + 3 * B_HEADS * HEAD_DIM
EVEN_OUT_ROWS = A_HEADS * A_V_DIM + B_HEADS * HEAD_DIM
ODD_WIDTH = C_HEADS * HEAD_DIM

kernel_name = "hybrid_mla_dilated_neighbourhood_encoder"

def rmsnorm(x, g):
    xf = x.astype(jnp.float32)
    y = xf * lax.rsqrt(jnp.mean(xf * xf, axis=-1, keepdims=True) + EPS)
    return (y * g.astype(jnp.float32)).astype(x.dtype)

def rope_tables(seq_len, dim):
    pos = jnp.arange(seq_len, dtype=jnp.float32)
    inv = ROPE_THETA ** (-jnp.arange(0, dim, 2, dtype=jnp.float32) / dim)
    ang = pos[:, None] * inv[None, :]
    return jnp.cos(ang), jnp.sin(ang)

def apply_rope(x, cos, sin):
    half = x.shape[-1] // 2
    shape = (x.shape[1],) + (1,) * (x.ndim - 3) + (half,)
    c = cos.reshape(shape).astype(x.dtype)
    s = sin.reshape(shape).astype(x.dtype)
    x1, x2 = x[..., :half], x[..., half:]
    return jnp.concatenate([x1 * c - x2 * s, x2 * c + x1 * s], axis=-1)

def softmax_with_lse(s):
    m = jnp.max(s, axis=-1, keepdims=True)
    e = jnp.exp(s - m)
    den = jnp.sum(e, axis=-1, keepdims=True)
    return e / den, (m + jnp.log(den))[..., 0]

def mla_attention(q_nope, q_pe, k_nope, k_pe, v):
    B, S, H, _ = q_nope.shape
    nb = S // Q_BLOCK
    scale = (A_NOPE_DIM + A_ROPE_DIM) ** -0.5

    def blocks(t):
        return t.reshape((B, nb, Q_BLOCK) + t.shape[2:]).swapaxes(0, 1)

    def one_block(args):
        qn, qp = args
        s = (jnp.einsum('bqhd,bkhd->bhqk', qn, k_nope)
             + jnp.einsum('bqhd,bkd->bhqk', qp, k_pe)).astype(jnp.float32) * scale
        p = jax.nn.softmax(s, axis=-1).astype(v.dtype)
        return jnp.einsum('bhqk,bkhd->bqhd', p, v)

    o = lax.map(one_block, (blocks(q_nope), blocks(q_pe)))
    return o.swapaxes(0, 1).reshape(B, S, H, v.shape[-1])

def banded_attention(q, k, v, half_window, scale):
    N, L, H, dh = q.shape
    blk = half_window
    nb = -(-L // blk)
    pad = nb * blk - L
    qb = jnp.pad(q, ((0, 0), (0, pad), (0, 0), (0, 0))).reshape(N, nb, blk, H, dh)

    def windows(t):
        tb = jnp.pad(t, ((0, 0), (blk, blk + pad), (0, 0), (0, 0))).reshape(N, nb + 2, blk, H, dh)
        return jnp.concatenate([tb[:, :-2], tb[:, 1:-1], tb[:, 2:]], axis=2)

    kw, vw = windows(k), windows(v)
    qpos = np.arange(nb)[:, None] * blk + np.arange(blk)[None, :]
    kpos = (np.arange(nb)[:, None] - 1) * blk + np.arange(3 * blk)[None, :]
    kp = kpos[:, None, :]
    valid = (np.abs(kp - qpos[:, :, None]) <= half_window) & (kp >= 0) & (kp < L)
    s = jnp.einsum('nbqhd,nbkhd->nbhqk', qb, kw).astype(jnp.float32) * scale
    s = jnp.where(valid[None, :, None], s, NEG_INF)
    p, lse = softmax_with_lse(s)
    o = jnp.einsum('nbhqk,nbkhd->nbqhd', p.astype(v.dtype), vw).reshape(N, nb * blk, H, dh)[:, :L]
    lse = lse.transpose(0, 1, 3, 2).reshape(N, nb * blk, H)[:, :L]
    return o, lse

def dilated_attention(q, k, v):
    B, S, H, dh = q.shape
    scale = dh ** -0.5
    outs, lses = [], []
    for window, dilation in B_BRANCHES:
        n_sub = S // dilation

        def to_sub(t):
            return t.reshape(B, n_sub, dilation, H, dh).swapaxes(1, 2).reshape(B * dilation, n_sub, H, dh)

        o, lse = banded_attention(to_sub(q), to_sub(k), to_sub(v), window // (2 * dilation), scale)
        outs.append(o.reshape(B, dilation, n_sub, H, dh).swapaxes(1, 2).reshape(B, S, H, dh))
        lses.append(lse.reshape(B, dilation, n_sub, H).swapaxes(1, 2).reshape(B, S, H))
    w = jax.nn.softmax(jnp.stack(lses), axis=0)
    return jnp.einsum('gbsh,gbshd->bshd', w.astype(q.dtype), jnp.stack(outs))

def neighbourhood_attention(q, k, v, rpb):
    B, S, H, dh = q.shape
    rows = S // GRID_W
    kr = min(NA_ROWS, rows)
    n_cb = GRID_W // NA_COL_BLOCK
    scale = dh ** -0.5
    r = np.arange(rows)
    row_start = np.clip(r - kr // 2, 0, rows - kr)
    row_off = row_start[:, None] + np.arange(kr)[None, :] - r[:, None] + (NA_ROWS - 1)
    qcol = np.arange(GRID_W).reshape(n_cb, NA_COL_BLOCK)
    col_start = np.clip(qcol - NA_COLS // 2, 0, GRID_W - NA_COLS)
    band_start = np.clip(np.arange(n_cb) * NA_COL_BLOCK - NA_COLS // 2, 0, GRID_W - NA_BAND)
    band_col = band_start[:, None] + np.arange(NA_BAND)[None, :]
    bc = band_col[:, None, :]
    col_valid = (bc >= col_start[..., None]) & (bc < col_start[..., None] + NA_COLS)
    col_off = np.clip(bc - qcol[..., None] + (NA_COLS - 1), 0, 2 * NA_COLS - 2)
    key_valid = np.broadcast_to(col_valid[:, :, None, :], (n_cb, NA_COL_BLOCK, kr, NA_BAND)).reshape(
        n_cb, NA_COL_BLOCK, kr * NA_BAND)
    kg = k.reshape(B, rows, GRID_W, H, dh)
    vg = v.reshape(B, rows, GRID_W, H, dh)
    qg = q.reshape(B, rows, GRID_W, H, dh).swapaxes(0, 1)

    def gather_band(t_rows):
        t = t_rows[:, :, band_col]
        return t.swapaxes(1, 2).reshape(B, n_cb, kr * NA_BAND, H, dh)

    def one_row(args):
        q_row, rs, ro = args
        k_band = gather_band(lax.dynamic_slice_in_dim(kg, rs, kr, axis=1))
        v_band = gather_band(lax.dynamic_slice_in_dim(vg, rs, kr, axis=1))
        q_blk = q_row.reshape(B, n_cb, NA_COL_BLOCK, H, dh)
        s = jnp.einsum('bjqhd,bjkhd->bhjqk', q_blk, k_band).astype(jnp.float32) * scale
        bias = rpb[:, ro[:, None, None, None], col_off[None]]
        bias = bias.transpose(0, 2, 3, 1, 4).reshape(H, n_cb, NA_COL_BLOCK, kr * NA_BAND)
        s = jnp.where(key_valid, s + bias.astype(jnp.float32), NEG_INF)
        p = jax.nn.softmax(s, axis=-1).astype(v.dtype)
        o = jnp.einsum('bhjqk,bjkhd->bjqhd', p, v_band)
        return o.reshape(B, GRID_W, H, dh)

    o = lax.map(one_row, (qg, jnp.asarray(row_start, jnp.int32), jnp.asarray(row_off, jnp.int32)))
    return o.swapaxes(0, 1).reshape(B, S, H, dh)

def even_mixer(h, w_in, q_norm, w_q_up, kv_norm, w_kv_up, w_out, cos_a, sin_a, cos_b, sin_b):
    B, S, _ = h.shape
    z = h @ w_in
    c_q, c_kv, k_pe, qkv_b = jnp.split(
        z, [A_Q_RANK, A_Q_RANK + A_KV_RANK, A_Q_RANK + A_KV_RANK + A_ROPE_DIM], axis=-1)
    q_a = (rmsnorm(c_q, q_norm) @ w_q_up).reshape(B, S, A_HEADS, A_NOPE_DIM + A_ROPE_DIM)
    q_nope = q_a[..., :A_NOPE_DIM]
    q_pe = apply_rope(q_a[..., A_NOPE_DIM:], cos_a, sin_a)
    kv = (rmsnorm(c_kv, kv_norm) @ w_kv_up).reshape(B, S, A_HEADS, A_NOPE_DIM + A_V_DIM)
    k_nope, v_a = kv[..., :A_NOPE_DIM], kv[..., A_NOPE_DIM:]
    k_pe = apply_rope(k_pe, cos_a, sin_a)
    o_a = mla_attention(q_nope, q_pe, k_nope, k_pe, v_a)
    qkv_b = qkv_b.reshape(B, S, 3, B_HEADS, HEAD_DIM)
    q_b = apply_rope(qkv_b[:, :, 0], cos_b, sin_b)
    k_b = apply_rope(qkv_b[:, :, 1], cos_b, sin_b)
    o_b = dilated_attention(q_b, k_b, qkv_b[:, :, 2])
    o = jnp.concatenate([o_a.reshape(B, S, A_HEADS * A_V_DIM), o_b.reshape(B, S, B_HEADS * HEAD_DIM)], axis=-1)
    return o @ w_out

def odd_mixer(h, w_qkv, rpb, w_out):
    B, S, _ = h.shape
    qkv = (h @ w_qkv).reshape(B, S, 3, C_HEADS, HEAD_DIM)
    o = neighbourhood_attention(qkv[:, :, 0], qkv[:, :, 1], qkv[:, :, 2], rpb)
    return o.reshape(B, S, ODD_WIDTH) @ w_out

def swiglu(h, w_gate, w_up, w_down):
    return (jax.nn.silu(h @ w_gate) * (h @ w_up)) @ w_down

def setup_inputs(seed: int = 0) -> dict:
    key = jax.random.key(seed)
    ks = jax.random.split(key, 20)
    f32 = jnp.float32

    def w(k, shape, fan_in):
        return jax.random.normal(k, shape, f32) * fan_in ** -0.5

    def gain(k, shape):
        return 1.0 + 0.05 * jax.random.normal(k, shape, f32)

    return {
        "x": jax.random.normal(ks[0], (BATCH, SEQ, D_MODEL), f32),
        "ev_norm": gain(ks[1], (N_EVEN, D_MODEL)),
        "ev_w_in": w(ks[2], (N_EVEN, D_MODEL, EVEN_IN_COLS), D_MODEL),
        "ev_q_norm": gain(ks[3], (N_EVEN, A_Q_RANK)),
        "ev_w_q_up": w(ks[4], (N_EVEN, A_Q_RANK, A_HEADS * (A_NOPE_DIM + A_ROPE_DIM)), A_Q_RANK),
        "ev_kv_norm": gain(ks[5], (N_EVEN, A_KV_RANK)),
        "ev_w_kv_up": w(ks[6], (N_EVEN, A_KV_RANK, A_HEADS * (A_NOPE_DIM + A_V_DIM)), A_KV_RANK),
        "ev_w_out": w(ks[7], (N_EVEN, EVEN_OUT_ROWS, D_MODEL), EVEN_OUT_ROWS),
        "od_norm": gain(ks[8], (N_ODD, D_MODEL)),
        "od_w_qkv": w(ks[9], (N_ODD, D_MODEL, 3 * ODD_WIDTH), D_MODEL),
        "od_rpb": 0.02 * jax.random.normal(ks[10], (N_ODD, C_HEADS, 2 * NA_ROWS - 1, 2 * NA_COLS - 1), f32),
        "od_w_out": w(ks[11], (N_ODD, ODD_WIDTH, D_MODEL), ODD_WIDTH),
        "ffn_norm": gain(ks[12], (DEPTH, D_MODEL)),
        "ffn_w_gate": w(ks[13], (DEPTH, D_MODEL, D_FF), D_MODEL),
        "ffn_w_up": w(ks[14], (DEPTH, D_MODEL, D_FF), D_MODEL),
        "ffn_w_down": w(ks[15], (DEPTH, D_FF, D_MODEL), D_FF),
        "final_norm": gain(ks[16], (D_MODEL,)),
    }

def reference(x, ev_norm, ev_w_in, ev_q_norm, ev_w_q_up, ev_kv_norm, ev_w_kv_up, ev_w_out,
              od_norm, od_w_qkv, od_rpb, od_w_out,
              ffn_norm, ffn_w_gate, ffn_w_up, ffn_w_down, final_norm):
    S = x.shape[1]
    cos_a, sin_a = rope_tables(S, A_ROPE_DIM)
    cos_b, sin_b = rope_tables(S, HEAD_DIM)
    h = x
    for layer in range(DEPTH):
        i = layer // 2
        if layer % 2 == 0:
            h = h + even_mixer(rmsnorm(h, ev_norm[i]), ev_w_in[i], ev_q_norm[i], ev_w_q_up[i],
                               ev_kv_norm[i], ev_w_kv_up[i], ev_w_out[i], cos_a, sin_a, cos_b, sin_b)
        else:
            h = h + odd_mixer(rmsnorm(h, od_norm[i]), od_w_qkv[i], od_rpb[i], od_w_out[i])
        h = h + swiglu(rmsnorm(h, ffn_norm[layer]), ffn_w_gate[layer], ffn_w_up[layer], ffn_w_down[layer])
    return rmsnorm(h, final_norm)


_drawn_inputs = setup_inputs


def setup_inputs(seed=0):
    import zlib

    import numpy as np

    out = dict(_drawn_inputs(seed))
    spreads = {}
    factors = {'ev_norm': 4.368,
     'ev_q_norm': 8.0,
     'ev_kv_norm': 6.103,
     'od_norm': 4.986,
     'od_rpb': 21.808}
    for name, (base, spread) in spreads.items():
        noise = np.random.default_rng([zlib.crc32(name.encode()), seed]).standard_normal(out[name].shape)
        drawn = base * np.exp(spread * noise) if base else spread * noise
        out[name] = __import__('jax').numpy.asarray(drawn.astype(out[name].dtype))
    for name, factor in factors.items():
        out[name] = (out[name] * factor).astype(out[name].dtype)
    return out
```

```python
from contextlib import ExitStack

import concourse.bass as bass
from concourse import mybir

F32 = mybir.dt.float32
F32R = mybir.dt.float32r
ALU = mybir.AluOpType
ACT = mybir.ActivationFunctionType
AX = mybir.AxisListType.X

P = 128
S = 512
DM = 1024
KT = DM // P
HD = 64
NOPE, ROPE = 64, 32
QA = NOPE + ROPE
QR, KVR = 256, 128
DFF = 2816
FT = DFF // P
A_PAIRS = B_PAIRS = 4
C_PAIRS = 8
RING = 4
EPS = 1e-6

STREAM = {
    "a0": (4, 8, 1, 32),
    "a": (2, 16, A_PAIRS, 6),
    "b": (3, 32, B_PAIRS, 24),
    "eo": (4, 16, 4, 16),
    "u0": (4, 4 * FT, FT, 16),
    "d0": (3, 64, 4, 2 * FT),
    "c": (3, 64, C_PAIRS, 24),
    "oo": (4, 16, 4, 16),
    "u1": (4, 4 * FT, FT, 16),
    "d1": (3, 64, 4, 2 * FT),
}
PER = {k: v[0] for k, v in STREAM.items()}
STEP_CHUNKS = {k: v[1] // v[2] for k, v in STREAM.items()}
STEP_TILES = {k: v[3] for k, v in STREAM.items()}
CHUNK0, TILE0 = {}, {}
_c = _t = 0
for _k, (_per, _n, _steps, _tiles) in STREAM.items():
    CHUNK0[_k], TILE0[_k] = _c, _t
    _c, _t = _c + _n, _t + _steps * _tiles


def through(phase, k):
    if phase == "a":
        return [2, 4, 5, 6][k]
    if phase in ("d0", "d1"):
        return (k // 8) * FT + min(3 * (k % 8 + 1), FT)
    return PER[phase] * (k + 1)


USED = [TILE0[ph] + st * STEP_TILES[ph] + through(ph, k)
        for ph, v in STREAM.items() for st in range(v[2]) for k in range(STEP_CHUNKS[ph])]

GAIN = {"ev": 0, "f0": 8, "od": 16, "f1": 24, "fin": 32, "q": 40, "kv": 42}
BAND_START = [0, 64, 192, 256]
BAND_KIND = [0, 1, 1, 2]
WIDE_OFF = [128, 64, 0]
BAND = 256
WIDE = 384


def build(nc, xT, gains, consts, tabA, tabB, lnc, cmask, bias, streams, out):
    ctx = ExitStack()
    with ctx:
        def sb(name, shape, dt=F32):
            return ctx.enter_context(nc.sbuf_tensor(name, shape, dt))

        def sem(name):
            return ctx.enter_context(nc.semaphore(name))

        x = sb("x_res", [P, KT, S])
        xn_hi = sb("xn_hi", [P, KT, S], F32R)
        xn_lo = sb("xn_lo", [P, KT, S], F32R)
        w_raw = sb("w_raw", [P, RING, 4 * P])
        w_hi = sb("w_hi", [P, RING, 4 * P], F32R)
        w_lo = sb("w_lo", [P, RING, 4 * P], F32R)
        shared = sb("shared", [P, 2 * FT * S], F32R)
        gain = sb("gain", [P, 48])
        cst = sb("cst", [P, 2, P])
        tabs = sb("tabs", [P, 10 * S])
        p = sb("p", [P, 4, S])
        rq = sb("rq", [P, S])
        rk = sb("rk", [P, S])
        sw = sb("sw", [P, S])
        vT = sb("vT", [P, S])
        to = sb("to", [P, S])
        of = sb("of", [P, S])
        acc = sb("acc", [P, S])
        small = sb("small", [P, 64])
        ps = ctx.enter_context(nc.psum_tensor("ps", [P, 8, S], F32))

        ident, ones = cst[:, 0, :], cst[:, 1, :]
        PJ, SC, PTB, OB = 0, 3, 5, 7
        mn, den, rden = small[:, 0:16], small[:, 16:32], small[:, 32:48]
        mean, root, rinv = small[:, 48:52], small[:, 52:56], small[:, 56:60]

        def part(off, n):
            return shared[:, off:off + n]

        q_hi = part(0, 2 * S).rearrange("p (h s) -> p h s", h=2)
        q_lo = part(2 * S, 2 * S).rearrange("p (h s) -> p h s", h=2)
        k_hi = part(4 * S, 2 * S).rearrange("p (h s) -> p h s", h=2)
        k_lo = part(6 * S, 2 * S).rearrange("p (h s) -> p h s", h=2)
        v_st = part(8 * S, 2 * S).rearrange("p (t h e d) -> p t h e d", t=4, h=2, e=2)
        pt_hi = part(10 * S, 4 * S)
        pt_lo = part(14 * S, 4 * S)
        cn_hi = part(18 * S, 3 * S).rearrange("p (k s) -> p k s", k=3)
        cn_lo = part(21 * S, 3 * S).rearrange("p (k s) -> p k s", k=3)
        v_sh = part(18 * S, 3 * S // 2).rearrange("p (t h e d) -> p t h e d", t=3, h=2, e=2)
        o_hi = part(24 * S, 8 * S).rearrange("p (k s) -> p k s", k=8)
        o_lo = part(32 * S, 8 * S).rearrange("p (k s) -> p k s", k=8)
        h_hi = part(0, FT * S).rearrange("p (k s) -> p k s", k=FT)
        h_lo = part(FT * S, FT * S).rearrange("p (k s) -> p k s", k=FT)

        tA = tabs[:, 0:2 * S].rearrange("p (k s) -> p k s", k=2)
        tB = tabs[:, 2 * S:6 * S].rearrange("p (k s) -> p k s", k=4)
        tM = tabs[:, 6 * S:10 * S].rearrange("p (k s) -> p k s", k=4)
        wide = tabs[:, 0:2 * WIDE].rearrange("p (h w) -> p h w", h=2)
        cm = tabs[:, 2 * WIDE:2 * WIDE + 3 * BAND].rearrange("p (k w) -> p k w", k=3)
        bt = tabs[:, 1536:1536 + 6 * BAND].rearrange("p (h k w) -> p h k w", h=2, k=3)

        landed = [sem(f"landed{s}") for s in range(RING)]
        x_landed, gain_landed, cst_landed, tabA_landed, tabB_landed, lnc_landed, cmask_landed, bias_landed, \
            vsh_landed, vsh2_landed = [sem(n) for n in (
                "x_landed gain_landed cst_landed tabA_landed tabB_landed lnc_landed cmask_landed bias_landed "
                "vsh_landed vsh2_landed").split()]
        tile_used, ss_done, rbc_done, score_done, pt_done, vt_done, pv_done = [sem(n) for n in (
            "tile_used ss_done rbc_done score_done pt_done vt_done pv_done").split()]
        w_hi_ready, square_done, root_done, xn_hi_done, exp_done, pt_hi_done, vT_done, v_hi_done, o1_done, \
            o_hi_done, c_done, swap_done, stage_hi_done, silu_done, hid_hi_done = [sem(n) for n in (
                "w_hi_ready square_done root_done xn_hi_done exp_done pt_hi_done vT_done v_hi_done o1_done "
                "o_hi_done c_done swap_done stage_hi_done silu_done hid_hi_done").split()]
        w_lo_ready, mean_done, diag_done, rinv_done, xf_done, min_done, rden_done, pt_lo_done, v_lo_done, o2_done, \
            rope_t_done, staged, kpe_done, pads_done, hid_done, res_done, fin_done, minima_go = [sem(n) for n in (
                "w_lo_ready mean_done diag_done rinv_done xf_done min_done rden_done pt_lo_done v_lo_done o2_done "
                "rope_t_done staged kpe_done pads_done hid_done res_done fin_done minima_go").split()]
        acc_zero, acc_done, xn_done, norm_done, rope_m_done, rope_done, o_lo_done, bias_ready, hid_lo_done = [
            sem(n) for n in (
                "acc_zero acc_done xn_done norm_done rope_m_done rope_done o_lo_done bias_ready hid_lo_done").split()]
        stored = sem("stored")

        CR_EXP, CR_PT, CR_PV, CR_PTL, CR_OLO, CR_SILU, CR_HID, CR_RES = 2, 4, 1, 2, 1, 1, 1, 2

        NORMS = ["ev", "q", "kv", "f0", "od", "f1", "fin"]
        WIDTH = {"ev": 8, "q": 2, "kv": 1, "f0": 8, "od": 8, "f1": 8, "fin": 8}
        END = {}
        n_tiles = 0
        for name in NORMS:
            n_tiles += WIDTH[name]
            END[name] = n_tiles

        def norm_src(name):
            if name == "q":
                return [rq[:], rk[:]]
            if name == "kv":
                return [vT[:]]
            return [x[:, k, :] for k in range(KT)]

        def norm_dst(name):
            if name == "q":
                return [(cn_hi[:, k, :], cn_lo[:, k, :]) for k in (0, 1)]
            if name == "kv":
                return [(cn_hi[:, 2, :], cn_lo[:, 2, :])]
            return [(xn_hi[:, k, :], xn_lo[:, k, :]) for k in range(KT)]

        LAG = 2
        SLOTS = {"a": 12, "b": 12, "c": 8}
        NTILES = {"a": 8, "b": 8, "c": 4}
        PV0 = {"a": 6, "b": 6, "c": 5}
        SPLITS = {"a": {1: 2, 2: 3}, "b": {0: 2, 2: 3, 3: 4, 5: 5, 6: 6, 8: 7}, "c": {0: 2, 1: 3, 2: 4, 3: 5, 4: 6, 5: 7}}
        Q0, Q1, KS, VS = "q0", "q1", "k", "v"

        block = ctx.enter_context(nc.Block())

        @block.sync
        def _(sp):
            for h in range(2):
                sp.dma_start(x[:, 4 * h:4 * h + 4, :], xT[:, 4 * h:4 * h + 4, :]).then_inc(x_landed, 16)
            sp.dma_start(gain[:], gains).then_inc(gain_landed, 16)
            sp.dma_start(cst[:], consts).then_inc(cst_landed, 16)
            for name in STREAM:
                per, n = STREAM[name][0:2]
                base, src = CHUNK0[name], streams[name]
                if name == "a0":
                    for c in range(n):
                        if c >= RING:
                            sp.wait_ge(w_lo_ready, c - RING + 1)
                        sp.dma_start(w_raw[:, c % RING, 0:per * P], src[c]).then_inc(landed[c % RING], 16)
                        if c == 3:
                            sp.dma_start(tA, tabA).then_inc(tabA_landed, 16)
                            sp.dma_start(tB, tabB).then_inc(tabB_landed, 16)
                            sp.dma_start(tM, lnc).then_inc(lnc_landed, 16)
                    continue
                with sp.Fori(0, n // RING) as i:
                    for s in range(RING):
                        sp.wait_ge(w_lo_ready, i * RING + (base + s - RING + 1))
                        sp.dma_start(w_raw[:, s, 0:per * P],
                                     src[bass.ds(i * RING + s, 1)].rearrange("c p w -> p (c w)")
                                     ).then_inc(landed[s], 16)
            for k in range(KT):
                sp.wait_ge(fin_done, k + 1)
                sp.dma_start(out[:, k, :], x[:, k, :]).then_inc(stored, 16)
            sp.wait_ge(stored, 16 * KT)

        @block.tensor
        def _(pe):
            mm = nc.tensor.matmul

            def weight_tile(phase, c0, n, bank, rhs, first, final, cols=P):
                per = PER[phase]
                if n % per == 0:
                    pe.wait_ge(w_lo_ready, c0 + (n // per + 1))
                s, o = (n // per) % RING, (n % per) * P
                a, b = w_hi[:, s, o:o + cols], w_lo[:, s, o:o + cols]
                r_hi, r_lo = rhs
                dst = ps[0:cols, bank, :]
                mm(dst, a, r_hi, start=first, stop=False)
                mm(dst, a, r_lo, start=False, stop=False)
                mm(dst, b, r_hi, start=False, stop=final).then_inc(tile_used, 1)

            def norm(n):
                name = NORMS[n]
                pe.wait_ge(acc_done, END[name])
                for t in range(4):
                    last = mm(ps[:, SC, t:t + 1], acc[:, t * P:(t + 1) * P], ones[:, 0:1], start=True, stop=True)
                last.then_inc(ss_done, 1)
                pe.wait_ge(diag_done, n + 1)
                for t in range(4):
                    last = mm(ps[:, SC + 1, t * P:(t + 1) * P], ones, of[:, t * P:(t + 1) * P],
                              start=True, stop=True)
                last.then_inc(rbc_done, 1)

            def xn(k):
                return xn_hi[:, k, :], xn_lo[:, k, :]

            def cn(k):
                return cn_hi[:, k, :], cn_lo[:, k, :]

            def values(pair):
                pe.wait_ge(vT_done, pair + 1)
                for t in range(4):
                    last = nc.tensor.transpose(ps[:, PJ + 2, t * P:(t + 1) * P], vT[:, t * P:(t + 1) * P], ident)
                last.then_inc(vt_done, 1)

            def scores(kind, tau, t):
                if kind == "a":
                    pe.wait_ge(exp_done, tau + (t + CR_EXP - 1))
                    rows, h, kh = QA, t // 4, t // 4
                else:
                    pe.wait_ge(min_done, tau + (t - 1))
                    rows, h, kh = P, t // (NTILES[kind] // 2), 0
                o = ps[:, SC + t % 2, :]
                if kind == "c":
                    for u in range(2):
                        j = 2 * (t % 2) + u
                        ou = o[:, u * BAND:(u + 1) * BAND]
                        qs, ks = slice(j * P, (j + 1) * P), slice(BAND_START[j], BAND_START[j] + BAND)
                        mm(ou, q_hi[:, h, qs], k_hi[:, 0, ks], start=True, stop=False)
                        mm(ou, q_hi[:, h, qs], k_lo[:, 0, ks], start=False, stop=False)
                        last = mm(ou, q_lo[:, h, qs], k_hi[:, 0, ks], start=False, stop=True)
                else:
                    qs = slice((t % 4) * P, (t % 4 + 1) * P)
                    mm(o, q_hi[0:rows, h, qs], k_hi[0:rows, kh, :], start=True, stop=False)
                    mm(o, q_hi[0:rows, h, qs], k_lo[0:rows, kh, :], start=False, stop=False)
                    last = mm(o, q_lo[0:rows, h, qs], k_hi[0:rows, kh, :], start=False, stop=True)
                last.then_inc(score_done, 1)

            def turn(tau, t):
                pe.wait_ge(norm_done, tau + (t + 1))
                pe.wait_ge(pt_lo_done, tau + (t + CR_PTL - 1))
                for kt in range(4):
                    last = nc.tensor.transpose(ps[:, PTB + t % 2, kt * P:(kt + 1) * P],
                                               p[:, t % 4, kt * P:(kt + 1) * P], ident)
                last.then_inc(pt_done, 1)

            def outputs(kind, pair, tau, h):
                pe.wait_ge(pt_lo_done, tau + (NTILES[kind] // 2 * (h + 1) + CR_PTL))
                pe.wait_ge(o2_done, pair * 2 + (h + 1))
                if h == 0:
                    pe.wait_ge(v_lo_done, pair + 1)
                if kind == "c":
                    if h == 0:
                        pe.wait_ge(vsh_landed, (pair - 7) * 16)
                        pe.wait_ge(vsh2_landed, (pair - 7) * 16)
                    for j in range(4):
                        o = ps[:, OB, j * P:(j + 1) * P]
                        for kt in range(2):
                            v = v_st[:, (j // 3) * 2 + kt, h] if j in (0, 3) else v_sh[:, j - 1 + kt, h]
                            v = v.rearrange("p e d -> p (e d)")
                            c = h * 2 * S + (j * 2 + kt) * P
                            mm(o, v, pt_hi[:, c:c + P], start=(kt == 0), stop=False)
                            last = mm(o, v, pt_lo[:, c:c + P], start=False, stop=(kt == 1))
                else:
                    for kt in range(4):
                        v = v_st[:, kt, h].rearrange("p e d -> p (e d)")
                        mm(ps[:, OB, :], v, pt_hi[:, kt * S:(kt + 1) * S], start=(kt == 0), stop=False)
                        last = mm(ps[:, OB, :], v, pt_lo[:, kt * S:(kt + 1) * S], start=False, stop=(kt == 3))
                last.then_inc(pv_done, 1)

            def project(kind, pair, c0, s):
                if kind == "a":
                    if s == 1:
                        for k in range(2):
                            weight_tile("a", c0, k, PJ, cn(k), k == 0, k == 1)
                    elif s == 2:
                        for k in range(2):
                            weight_tile("a", c0, 2 + k, PJ + 1, cn(k), k == 0, k == 1)
                    elif s == 4:
                        if not isinstance(pair, int) or pair > 0:
                            pe.wait_ge(v_lo_done, pair)
                        weight_tile("a", c0, 4, PJ + 2, cn(2), True, True)
                    elif s == 7:
                        pe.wait_ge(vT_done, pair + 1)
                        weight_tile("a", c0, 6, PJ + 2, cn(2), True, True)
                    return
                n = 24 // SLOTS[kind]
                for m in range(n * s, n * (s + 1)):
                    if m == 16:
                        pe.wait_ge(v_lo_done, pair)
                    weight_tile(kind, c0, m, PJ + m // KT, xn(m % KT), m % KT == 0, m % KT == KT - 1)

            def heads(kind, pair, tau, c0):
                pe.wait_ge(staged, pair + 1)
                for s in range(SLOTS[kind]):
                    if s < NTILES[kind]:
                        if kind == "b" and s == 0:
                            pe.wait_ge(exp_done, 8 * A_PAIRS + CR_EXP)
                        scores(kind, tau, s)
                    if s == 1:
                        values(pair)
                    if s == PV0[kind]:
                        outputs(kind, pair, tau, 0)
                    if c0 is not None:
                        project(kind, pair + 1, c0, s)
                    if LAG <= s < NTILES[kind] + LAG:
                        turn(tau, s - LAG)
                outputs(kind, pair, tau, 1)

            def pairs(kind, pair0, n, tau0):
                for s in range(SLOTS[kind]):
                    project(kind, pair0, CHUNK0[kind], s)
                with pe.Fori(0, n - 1) as i:
                    heads(kind, i + pair0, i * NTILES[kind] + tau0, i * STEP_CHUNKS[kind] + (CHUNK0[kind] + STEP_CHUNKS[kind]))
                heads(kind, pair0 + n - 1, tau0 + (n - 1) * NTILES[kind], None)

            def columns(phase, m0, nk, rhs):
                with pe.Fori(0, 4) as i:
                    for u in range(2):
                        pe.wait_ge(res_done, i * 2 + (m0 + u + 1))
                        for k in range(nk):
                            n = u * PER[phase] * STEP_CHUNKS[phase] // 2 + k
                            weight_tile(phase, i * STEP_CHUNKS[phase] + CHUNK0[phase], n, PTB + u, rhs(k), k == 0,
                                        k == nk - 1)

            def ffn(layer):
                phase = f"u{layer}"
                with pe.Fori(0, FT) as f:
                    for g in range(2):
                        free = (silu_done, CR_SILU) if g == 0 else (hid_done, CR_HID)
                        pe.wait_ge(free[0], f + (layer * FT + free[1]))
                        for k in range(KT):
                            weight_tile(phase, f * 4 + CHUNK0[phase], g * KT + k, g, xn(k), k == 0, k == KT - 1)
                pe.wait_ge(hid_lo_done, (layer + 1) * FT)
                columns(f"d{layer}", 8 + 16 * layer, FT, lambda k: (h_hi[:, k, :], h_lo[:, k, :]))

            pe.sem_inc(pt_done, CR_PT)
            pe.sem_inc(pv_done, CR_PV)
            pe.wait_ge(cst_landed, 16)
            norm(0)
            for m in range(4):
                for k in range(KT):
                    if m == 0:
                        pe.wait_ge(xn_done, k + 1)
                    weight_tile("a0", 0, m * KT + k, (PJ, PJ + 1, PJ + 2, OB)[m], xn(k), k == 0, k == KT - 1,
                                cols=P if m < 3 else 2 * ROPE)
            norm(1)
            norm(2)
            pe.wait_ge(xn_done, END["kv"])
            pairs("a", 0, A_PAIRS, 0)
            pairs("b", A_PAIRS, B_PAIRS, 8 * A_PAIRS)
            pe.wait_ge(o_lo_done, 8 + CR_OLO)
            columns("eo", 0, KT, lambda k: (o_hi[:, k, :], o_lo[:, k, :]))
            norm(3)
            pe.wait_ge(xn_done, END["f0"])
            ffn(0)
            norm(4)
            pe.wait_ge(xn_done, END["od"])
            pairs("c", 8, C_PAIRS, 8 * (A_PAIRS + B_PAIRS))
            pe.wait_ge(o_lo_done, 16 + CR_OLO)
            columns("oo", 16, KT, lambda k: (o_hi[:, k, :], o_lo[:, k, :]))
            norm(5)
            pe.wait_ge(xn_done, END["f1"])
            ffn(1)
            norm(6)

        @block.scalar
        def _(act):
            def copy(out, in_, scale=1.0):
                return nc.scalar.activation(out, in_, ACT.Copy, scale=scale)

            def split(phase, step, k):
                per, w = PER[phase], PER[phase] * P
                c = step * STEP_CHUNKS[phase] + (CHUNK0[phase] + k)
                act.wait_ge(landed[k % RING], chunk_bytes(phase, step, k))
                if isinstance(step, int):
                    if c >= RING:
                        act.wait_ge(tile_used, USED[c - RING])
                else:
                    K = STEP_CHUNKS[phase]
                    j = k - RING
                    back = through(phase, j) if j >= 0 else through(phase, j + K) - STEP_TILES[phase]
                    act.wait_ge(tile_used, step * STEP_TILES[phase] + (TILE0[phase] + back))
                copy(w_hi[:, k % RING, 0:w], w_raw[:, k % RING, 0:w]).then_inc(w_hi_ready, 1)

            def chunk_bytes(phase, step, k):
                K = STEP_CHUNKS[phase]
                return step * (16 * K // RING) + 16 * ((CHUNK0[phase] + k) // RING + 1)

            def square(src, n):
                if n >= 1:
                    act.wait_ge(acc_done, n)
                nc.scalar.activation(sw[:], src, ACT.Square).then_inc(square_done, 1)

            def norm(n):
                name = NORMS[n]
                act.wait_ge(mean_done, n + 1)
                nc.scalar.activation(root, mean, ACT.Sqrt).then_inc(root_done, 1)
                if name == "fin":
                    return
                g0 = END[name] - WIDTH[name]
                for k, (hi, lo) in enumerate(norm_dst(name)):
                    act.wait_ge(xf_done, g0 + k + 1)
                    copy(hi, p[:, (g0 + k) % 4, :]).then_inc(xn_hi_done, 1)

            def exps(kind, tau, t):
                act.wait_ge(min_done, tau + (t + 1))
                if kind == "a":
                    act.wait_ge(pt_done, tau + (t + 1))
                    nc.scalar.activation(p[:, t % 4, :], ps[:, SC + t % 2, :], ACT.Exp, bias=mn[:, t:t + 1], scale=-1.0,
                                         accum_out=den[:, t:t + 1]).then_inc(exp_done, 1)
                    return
                n = 2 if kind == "c" else 1
                w = S // n
                for u in range(n):
                    c = n * t + u
                    pu = p[:, t % 4, u * w:(u + 1) * w]
                    last = nc.scalar.activation(pu, pu, ACT.Exp, bias=mn[:, c:c + 1], scale=-1.0,
                                                accum_out=den[:, c:c + 1])
                last.then_inc(exp_done, 1)

            def turned(kind, pair, tau, t):
                act.wait_ge(pt_done, tau + (t + 1 + CR_PT))
                half = NTILES[kind] // 2
                if t % half == 0:
                    act.wait_ge(pv_done, pair * 2 + (t // half + (1 if kind != "c" else 0)))
                src = ps[:, PTB + t % 2, :]
                if kind == "c":
                    copy(pt_hi[:, t * S:(t + 1) * S], src).then_inc(pt_hi_done, 1)
                else:
                    dst = pt_hi.rearrange("p (k s) -> p k s", k=4)[:, :, (t % 4) * P:(t % 4 + 1) * P]
                    copy(dst, src.rearrange("p (k s) -> p k s", k=4)).then_inc(pt_hi_done, 1)

            def out_low(pair, h):
                act.wait_ge(pv_done, pair * 2 + (h + 1 + CR_PV))
                copy(to[h * HD:(h + 1) * HD, :], ps[HD:P, OB, :]).then_inc(o1_done, 1)

            def out_high(kind, pair):
                act.wait_ge(o2_done, pair * 2 + 3)
                k = pair - 8 if kind == "c" else pair
                copy(o_hi[:, bass.ds(k, 1), :], of[:].rearrange("p (k s) -> p k s", k=1)).then_inc(o_hi_done, 1)

            def values_high(pair):
                act.wait_ge(vt_done, pair + 1)
                src = ps[:, PJ + 2, :].rearrange("p (t h d) -> p t h d", t=4, h=2)
                copy(v_st[:, :, :, 0, :], src).then_inc(v_hi_done, 1)

            def shift_values(pair):
                act.wait_ge(v_lo_done, pair + 1)
                flat = v_st.rearrange("p t h e d -> p t (h e d)")
                dst = v_sh.rearrange("p t h e d -> p t (h e d)")
                act.dma_start(dst[0:HD].bitcast(F32), flat[HD:P, 0:3].bitcast(F32)).then_inc(vsh_landed, 16)
                act.dma_start(dst[HD:P].bitcast(F32), flat[0:HD, 1:4].bitcast(F32)).then_inc(vsh2_landed, 16)

            def project(kind, pair, step, s):
                if s in SPLITS[kind]:
                    split(kind, step, SPLITS[kind][s])

                def tiles(n):
                    act.wait_ge(tile_used, step * STEP_TILES[kind] + (TILE0[kind] + n))

                def q_k_free():
                    if not (isinstance(pair, int) and pair in (0, 4, 8)):
                        act.wait_ge(score_done, free_tau(kind, pair))
                    elif pair == 4:
                        act.wait_ge(score_done, 8 * A_PAIRS)
                        act.wait_ge(pads_done, 1)
                    elif pair == 8:
                        act.wait_ge(pads_done, 2)

                if kind == "a":
                    if s == 5:
                        tiles(5)
                        copy(vT[:], ps[:, PJ + 2, :]).then_inc(vT_done, 1)
                    if s == 9:
                        q_k_free()
                        act.wait_ge(rope_done, pair * 2 + 2)
                        for h, src in enumerate((rq, rk)):
                            copy(q_hi[0:QA, h, :], src[0:QA, :])
                        tiles(6)
                        for h in range(2):
                            last = copy(k_hi[0:NOPE, h, :], ps[h * NOPE:(h + 1) * NOPE, PJ + 2, :])
                        last.then_inc(stage_hi_done, 1)
                elif kind == "b":
                    if s in (4, 8):
                        m = 0 if s == 4 else 1
                        tiles(8 * (m + 1))
                        act.wait_ge(rope_done, pair * 2 + m)
                        act.wait_ge(rope_t_done, pair * 2 + (m + 1))
                        for g in range(4):
                            last = copy(sw[32 * g:32 * g + 32, :], ps[32 * (g ^ 1):32 * (g ^ 1) + 32, PJ + m, :])
                        last.then_inc(swap_done, 1)
                    if s == 9:
                        q_k_free()
                        act.wait_ge(rope_done, pair * 2 + 1)
                        for h in range(2):
                            last = copy(q_hi[h * HD:(h + 1) * HD, h, :], rq[h * HD:(h + 1) * HD, :])
                        last.then_inc(stage_hi_done, 1)
                    if s == 10:
                        act.wait_ge(rope_done, pair * 2 + 2)
                        copy(k_hi[:, 0, :], rk[:]).then_inc(stage_hi_done, 1)
                    if s == 12:
                        tiles(24)
                        copy(vT[:], ps[:, PJ + 2, :]).then_inc(vT_done, 1)
                else:
                    if s == 4:
                        q_k_free()
                        tiles(8)
                        for h in range(2):
                            last = copy(q_hi[h * HD:(h + 1) * HD, h, :], ps[h * HD:(h + 1) * HD, PJ, :], -HD ** -0.5)
                        last.then_inc(stage_hi_done, 1)
                    if s == 6:
                        tiles(16)
                        copy(k_hi[:, 0, :], ps[:, PJ + 1, :]).then_inc(stage_hi_done, 1)
                    if s == 8:
                        tiles(24)
                        copy(vT[:], ps[:, PJ + 2, :]).then_inc(vT_done, 1)

            def heads(kind, pair, tau, step):
                if step is not None:
                    split(kind, step, 0)
                    split(kind, step, 1)
                for s in range(SLOTS[kind]):
                    if s < NTILES[kind]:
                        exps(kind, tau, s)
                    if s == 2:
                        values_high(pair)
                    if kind == "c" and s == 3:
                        shift_values(pair)
                    if LAG <= s < NTILES[kind] + LAG:
                        turned(kind, pair, tau, s - LAG)
                    if s == PV0[kind] + 1:
                        out_low(pair, 0)
                    if step is not None:
                        project(kind, pair + 1, step, s)
                if step is not None:
                    project(kind, pair + 1, step, SLOTS[kind])
                out_low(pair, 1)
                out_high(kind, pair)

            def free_tau(kind, pair):
                return pair * 8 if kind != "c" else (pair - 8) * 4 + 64

            def pairs(kind, pair0, n, tau0):
                split(kind, 0, 0)
                split(kind, 0, 1)
                for s in range(SLOTS[kind] + 1):
                    project(kind, pair0, 0, s)
                with act.Fori(0, n - 1) as i:
                    heads(kind, i + pair0, i * NTILES[kind] + tau0, i + 1)
                heads(kind, pair0 + n - 1, tau0 + (n - 1) * NTILES[kind], None)

            def columns(phase, m0, sq0):
                K = STEP_CHUNKS[phase]

                def step(i, before):
                    for k in range(K):
                        split(phase, i, k)
                        if k == 1 and before:
                            added(i * 2 - 1)
                        if k == K // 2 + 1:
                            added(i * 2)

                def added(m):
                    act.wait_ge(res_done, m + (m0 + 1 + CR_RES))
                    act.wait_ge(acc_done, m + sq0)
                    nc.scalar.activation(sw[:].rearrange("p (k s) -> p k s", k=1), x[:, bass.ds(m, 1), :],
                                         ACT.Square).then_inc(square_done, 1)

                step(0, False)
                with act.Fori(1, 4) as i:
                    step(i, True)
                added(7)

            def ffn(layer):
                phase = f"u{layer}"

                def silu(f):
                    act.wait_ge(tile_used, f * 16 + (TILE0[phase] + 8))
                    act.wait_ge(hid_done, f + (layer * FT + CR_HID))
                    nc.scalar.activation(rq[:], ps[:, 0, :], ACT.Silu).then_inc(silu_done, 1)

                def hidden(f):
                    act.wait_ge(hid_done, f + (layer * FT + 1 + CR_HID))
                    copy(h_hi[:, bass.ds(f, 1), :], rk[:].rearrange("p (k s) -> p k s", k=1)).then_inc(hid_hi_done, 1)

                def step(f, before):
                    split(phase, f, 0)
                    split(phase, f, 1)
                    if before:
                        hidden(f - 1)
                    split(phase, f, 2)
                    split(phase, f, 3)
                    silu(f)

                step(0, False)
                with act.Fori(1, FT) as f:
                    step(f, True)
                hidden(FT - 1)
                columns(f"d{layer}", 8 + 16 * layer, END["f0" if layer == 0 else "f1"])

            act.sem_inc(exp_done, CR_EXP)
            act.sem_inc(silu_done, CR_SILU)
            for k in range(KT):
                act.wait_ge(x_landed, 32)
                square(x[:, k, :], k)
            split("a0", 0, 0)
            split("a0", 0, 1)
            split("a0", 0, 2)
            norm(0)
            for k in range(3, 8):
                split("a0", 0, k)
                if k in (5, 6, 7):
                    m = k - 5
                    act.wait_ge(tile_used, 8 * (m + 1))
                    square(ps[:, PJ + m, :], 8 + m)
                    copy((rq, rk, vT)[m][:], ps[:, PJ + m, :]).then_inc(c_done, 1)
            act.wait_ge(kpe_done, 3)
            for h in range(2):
                last = copy(k_hi[NOPE:QA, h, :], of[NOPE:QA, :])
            last.then_inc(stage_hi_done, 1)
            norm(1)
            norm(2)
            pairs("a", 0, A_PAIRS, 0)
            pairs("b", A_PAIRS, B_PAIRS, 8 * A_PAIRS)
            columns("eo", 0, END["kv"])
            norm(3)
            ffn(0)
            norm(4)
            pairs("c", 8, C_PAIRS, 8 * (A_PAIRS + B_PAIRS))
            columns("oo", 16, END["od"])
            norm(5)
            ffn(1)
            norm(6)

        @block.vector
        def _(dve):
            tt, sub, mul, add = nc.vector.tensor_tensor, ALU.subtract, ALU.mult, ALU.add

            def low(out, full, high):
                return tt(out, full, high.bitcast(F32), sub)

            def split(phase, step, k):
                w = PER[phase] * P
                dve.wait_ge(w_hi_ready, step * STEP_CHUNKS[phase] + (CHUNK0[phase] + k + 1))
                low(w_lo[:, k % RING, 0:w], w_raw[:, k % RING, 0:w], w_hi[:, k % RING, 0:w]).then_inc(w_lo_ready, 1)

            def norm(n):
                name = NORMS[n]
                dve.wait_ge(ss_done, n + 1)
                nc.vector.tensor_scalar(mean, ps[:, SC, 0:4], 1.0 / (WIDTH[name] * P), EPS, mul, add).then_inc(mean_done, 1)
                dve.wait_ge(root_done, n + 1)
                nc.vector.reciprocal(rinv, root).then_inc(rinv_done, 1)
                dve.wait_ge(rinv_done, n + 1)
                tt(of[:].rearrange("p (t s) -> p t s", t=4), ident.unsqueeze(1).to_broadcast([P, 4, P]),
                   rinv.unsqueeze(2).to_broadcast([P, 4, P]), mul).then_inc(diag_done, 1)
                dve.wait_ge(rbc_done, n + 1)
                g0 = END[name] - WIDTH[name]
                for k, src in enumerate(norm_src(name)):
                    gk = gain[:, GAIN[name] + k:GAIN[name] + k + 1]
                    if name == "fin":
                        nc.vector.scalar_tensor_tensor(out=src, in0=src, scalar=gk, in1=ps[:, SC + 1, :], op0=mul,
                                                       op1=mul).then_inc(fin_done, 1)
                        continue
                    if g0 + k >= 4:
                        dve.wait_ge(xn_done, g0 + k - 3)
                    nc.vector.scalar_tensor_tensor(out=p[:, (g0 + k) % 4, :], in0=src, scalar=gk, in1=ps[:, SC + 1, :],
                                                   op0=mul, op1=mul).then_inc(xf_done, 1)

            def minima(kind, pair, tau, t):
                dve.wait_ge(score_done, tau + (t + 1))
                o = ps[:, SC + t % 2, :]
                if kind == "a":
                    nc.vector.tensor_reduce(mn[:, t:t + 1], o, AX, ALU.min).then_inc(min_done, 1)
                    return
                dve.wait_ge(pt_done, tau + (t + 1))
                n = 2 if kind == "c" else 1
                w = S // n
                if kind == "c" and t % 2 == 0:
                    dve.wait_ge(bias_ready, (pair - 8) * 2 + (t // 2 + 1))
                dve.sem_inc(minima_go, 1)
                for u in range(n):
                    table = tM[:, t % 4, :] if kind == "b" else bt[:, t // 2, BAND_KIND[2 * (t % 2) + u], :]
                    c = n * t + u
                    last = nc.vector.tensor_tensor_reduce(
                        out=p[:, t % 4, u * w:(u + 1) * w], in0=o[:, u * w:(u + 1) * w], in1=table, scale=1.0,
                        scalar=3.0e38, op0=add, op1=ALU.min, accum_out=mn[:, c:c + 1])
                last.then_inc(min_done, 1)

            def inverse(kind, tau, t):
                dve.wait_ge(exp_done, tau + (t + 1 + CR_EXP))
                n = 2 if kind == "c" else 1
                nc.vector.reciprocal(rden[:, n * t:n * t + n], den[:, n * t:n * t + n]).then_inc(rden_done, 1)

            def turned(kind, tau, t):
                dve.wait_ge(pt_hi_done, tau + (t + 1))
                src = ps[:, PTB + t % 2, :]
                if kind == "c":
                    sl = slice(t * S, (t + 1) * S)
                    low(pt_lo[:, sl], src, pt_hi[:, sl]).then_inc(pt_lo_done, 1)
                else:
                    qs = slice((t % 4) * P, (t % 4 + 1) * P)
                    low(pt_lo.rearrange("p (k s) -> p k s", k=4)[:, :, qs], src.rearrange("p (k s) -> p k s", k=4),
                        pt_hi.rearrange("p (k s) -> p k s", k=4)[:, :, qs]).then_inc(pt_lo_done, 1)

            def out_sum(pair, h):
                dve.wait_ge(o1_done, pair * 2 + (h + 1))
                if h == 0:
                    dve.wait_ge(o_lo_done, pair + CR_OLO)
                r = slice(h * HD, (h + 1) * HD)
                tt(of[r, :], ps[0:HD, OB, :], to[r, :], add).then_inc(o2_done, 1)

            def values_low(pair):
                dve.wait_ge(v_hi_done, pair + 1)
                src = ps[:, PJ + 2, :].rearrange("p (t h d) -> p t h d", t=4, h=2)
                low(v_st[:, :, :, 1, :], src, v_st[:, :, :, 0, :]).then_inc(v_lo_done, 1)

            def project(kind, pair, step, s):
                if s in SPLITS[kind]:
                    split(kind, step, SPLITS[kind][s])

                def tiles(n):
                    dve.wait_ge(tile_used, step * STEP_TILES[kind] + (TILE0[kind] + n))

                def stage_hi(n):
                    base = {"a": (1, 1), "b": (2, 1 + A_PAIRS - 2 * 4), "c": (2, 1 + A_PAIRS + 2 * B_PAIRS - 2 * 8)}[kind]
                    dve.wait_ge(stage_hi_done, pair * base[0] + (base[1] + n))

                if kind == "a":
                    if s in (2, 3):
                        h, dst = s - 2, (rq, rk)[s - 2]
                        tiles(2 * (h + 1))
                        tt(dst[0:QA, :], ps[0:QA, PJ + h, :], tA[0:QA, 0, :], mul)
                        if h == 1:
                            dve.wait_ge(rope_done, pair * 2 + 1)
                        tt(sw[NOPE:QA, :], ps[QA:P, PJ + h, :], tA[NOPE:QA, 1, :], mul).then_inc(rope_t_done, 1)
                        dve.wait_ge(rope_t_done, pair * 2 + (h + 1))
                        tt(dst[NOPE:QA, :], dst[NOPE:QA, :], sw[NOPE:QA, :], add).then_inc(rope_done, 1)
                    if s == 10:
                        stage_hi(1)
                        for h, src in enumerate((rq, rk)):
                            low(q_lo[0:QA, h, :], src[0:QA, :], q_hi[0:QA, h, :])
                        for h in range(2):
                            last = low(k_lo[0:NOPE, h, :], ps[h * NOPE:(h + 1) * NOPE, PJ + 2, :], k_hi[0:NOPE, h, :])
                        last.then_inc(staged, 1)
                elif kind == "b":
                    if s in (4, 8):
                        m = 0 if s == 4 else 1
                        tiles(8 * (m + 1))
                        tt((rq, rk)[m][:], ps[:, PJ + m, :], tB[:, 2 * m, :], mul).then_inc(rope_t_done, 1)
                    if s == 10:
                        stage_hi(1)
                        for h in range(2):
                            r = slice(h * HD, (h + 1) * HD)
                            low(q_lo[r, h, :], rq[r, :], q_hi[r, h, :])
                    if s == 11:
                        stage_hi(2)
                        low(k_lo[:, 0, :], rk[:], k_hi[:, 0, :]).then_inc(staged, 1)
                else:
                    if s == 4:
                        stage_hi(1)
                        for h in range(2):
                            r = slice(h * HD, (h + 1) * HD)
                            nc.vector.scalar_tensor_tensor(out=q_lo[r, h, :], in0=ps[r, PJ, :], scalar=-HD ** -0.5,
                                                           in1=q_hi[r, h, :].bitcast(F32), op0=mul, op1=sub)
                    if s == 6:
                        stage_hi(2)
                        low(k_lo[:, 0, :], ps[:, PJ + 1, :], k_hi[:, 0, :]).then_inc(staged, 1)

            def heads(kind, pair, tau, step):
                if step is not None:
                    split(kind, step, 0)
                    split(kind, step, 1)
                for s in range(SLOTS[kind]):
                    if s < NTILES[kind]:
                        minima(kind, pair, tau, s)
                    if 1 <= s <= NTILES[kind]:
                        inverse(kind, tau, s - 1)
                    if s == 2:
                        values_low(pair)
                    if LAG <= s < NTILES[kind] + LAG:
                        turned(kind, tau, s - LAG)
                    if s == PV0[kind] + 1:
                        out_sum(pair, 0)
                    if step is not None:
                        project(kind, pair + 1, step, s)
                out_sum(pair, 1)

            def pads():
                for t in (q_hi, q_lo):
                    nc.vector.memset(t[HD:P, 0, :].bitcast(F32), 0.0)
                    last = nc.vector.memset(t[0:HD, 1, :].bitcast(F32), 0.0)
                last.then_inc(pads_done, 1)

            def pairs(kind, pair0, n, tau0):
                split(kind, 0, 0)
                split(kind, 0, 1)
                for s in range(SLOTS[kind]):
                    project(kind, pair0, 0, s)
                with dve.Fori(0, n - 1) as i:
                    heads(kind, i + pair0, i * NTILES[kind] + tau0, i + 1)
                heads(kind, pair0 + n - 1, tau0 + (n - 1) * NTILES[kind], None)

            def columns(phase, nk):
                K = STEP_CHUNKS[phase]

                def added(m, u):
                    dve.wait_ge(tile_used, m * nk + (TILE0[phase] + nk))
                    xm = x[:, bass.ds(m, 1), :]
                    tt(xm, ps[:, PTB + u, :].rearrange("p (k s) -> p k s", k=1), xm, add).then_inc(res_done, 1)

                def step(i, before):
                    for k in range(K):
                        split(phase, i, k)
                        if k == 1 and before:
                            added(i * 2 - 1, 1)
                        if k == K // 2 + 1:
                            added(i * 2, 0)

                step(0, False)
                with dve.Fori(1, 4) as i:
                    step(i, True)
                added(7, 1)

            def ffn(layer):
                phase = f"u{layer}"

                def hidden(f):
                    dve.wait_ge(silu_done, f + (layer * FT + 1 + CR_SILU))
                    dve.wait_ge(tile_used, f * 16 + (TILE0[phase] + 16))
                    if not isinstance(f, int) or f + layer > 0:
                        dve.wait_ge(hid_lo_done, f + layer * FT)
                    tt(rk[:], ps[:, 1, :], rq[:], mul).then_inc(hid_done, 1)

                def step(f, before):
                    split(phase, f, 0)
                    split(phase, f, 1)
                    if before == "first":
                        hidden(0)
                    elif before:
                        hidden(f - 1)
                    split(phase, f, 2)
                    split(phase, f, 3)

                step(0, False)
                step(1, "first")
                with dve.Fori(2, FT) as f:
                    step(f, True)
                hidden(FT - 1)
                columns(f"d{layer}", FT)

            dve.sem_inc(pt_lo_done, CR_PTL)
            dve.sem_inc(hid_done, CR_HID)
            dve.sem_inc(res_done, CR_RES)
            for k in range(3):
                split("a0", 0, k)
            dve.wait_ge(gain_landed, 16)
            dve.wait_ge(cst_landed, 16)
            norm(0)
            for k in range(3, 8):
                split("a0", 0, k)
            dve.wait_ge(tabA_landed, 16)
            dve.wait_ge(tile_used, 32)
            r = slice(NOPE, QA)
            tt(to[r, :], ps[0:ROPE, OB, :], tA[0:ROPE, 1, :], mul).then_inc(kpe_done, 1)
            tt(of[r, :], ps[ROPE:2 * ROPE, OB, :], tA[QA:P, 0, :], mul).then_inc(kpe_done, 1)
            dve.wait_ge(kpe_done, 2)
            tt(of[r, :], to[r, :], of[r, :], add).then_inc(kpe_done, 1)
            dve.wait_ge(stage_hi_done, 1)
            for h in range(2):
                last = low(k_lo[r, h, :], of[r, :], k_hi[r, h, :])
            last.then_inc(o2_done, 1)
            dve.wait_ge(c_done, 3)
            norm(1)
            norm(2)
            pairs("a", 0, A_PAIRS, 0)
            dve.wait_ge(score_done, 8 * A_PAIRS)
            pads()
            dve.wait_ge(tabB_landed, 16)
            dve.wait_ge(lnc_landed, 16)
            pairs("b", A_PAIRS, B_PAIRS, 8 * A_PAIRS)
            columns("eo", KT)
            norm(3)
            ffn(0)
            norm(4)
            pads()
            pairs("c", 8, C_PAIRS, 8 * (A_PAIRS + B_PAIRS))
            columns("oo", KT)
            norm(5)
            ffn(1)
            norm(6)

        @block.gpsimd
        def _(pool):
            tt, sub, mul, add = nc.gpsimd.tensor_tensor, ALU.subtract, ALU.mult, ALU.add

            def square_add(n):
                pool.wait_ge(square_done, n + 1)
                if not isinstance(n, int) or n >= 1:
                    pool.wait_ge(acc_done, n)
                tt(acc[:], acc[:], sw[:], add).then_inc(acc_done, 1)

            def clear(n):
                pool.wait_ge(ss_done, n + 1)
                nc.gpsimd.memset(acc[:], 0.0).then_inc(acc_zero, 1)
                pool.wait_ge(acc_zero, n + 2)

            def norm_low(n):
                name = NORMS[n]
                g0 = END[name] - WIDTH[name]
                for k, (hi, lo) in enumerate(norm_dst(name)):
                    pool.wait_ge(xn_hi_done, g0 + k + 1)
                    tt(lo, p[:, (g0 + k) % 4, :], hi.bitcast(F32), sub).then_inc(xn_done, 1)

            def normalise(kind, tau, t):
                pool.wait_ge(rden_done, tau + (t + 1))
                n = 2 if kind == "c" else 1
                pu = p[:, t % 4, :].rearrange("p (n w) -> p n w", n=n)
                r = rden[:, n * t:n * t + n].unsqueeze(2).to_broadcast([P, n, S // n])
                tt(pu, pu, r, mul).then_inc(norm_done, 1)

            def biases(pair, h):
                for kind in range(3):
                    last = tt(bt[:, h, kind, :], cm[:, kind, :], wide[:, h, WIDE_OFF[kind]:WIDE_OFF[kind] + BAND], sub)
                last.then_inc(bias_ready, 1)

            def load_biases(pair):
                pool.dma_start(wide, bias[bass.ds((pair - 8) * 2, 2)].rearrange("h p w -> p h w")).then_inc(bias_landed, 16)

            def project(kind, pair, tau, s):
                if kind == "b" and s in (5, 9):
                    m = 0 if s == 5 else 1
                    pool.wait_ge(swap_done, (pair - 4) * 2 + (m + 1))
                    tt(sw[:], sw[:], tB[:, 2 * m + 1, :], mul).then_inc(rope_m_done, 1)
                    pool.wait_ge(rope_m_done, (pair - 4) * 2 + (m + 1))
                    pool.wait_ge(rope_t_done, pair * 2 + (m + 1))
                    dst = (rq, rk)[m][:]
                    tt(dst, dst, sw[:], add).then_inc(rope_done, 1)
                if kind == "c" and s == 0:
                    pool.wait_ge(bias_ready, (pair - 8) * 2)
                    load_biases(pair)
                if kind == "c" and s in (4, 5):
                    h = s - 4
                    pool.wait_ge(bias_landed, (pair - 7) * 16)
                    pool.wait_ge(min_done, tau + 2 * (h + 1))
                    biases(pair, h)

            def heads(kind, pair, tau, more):
                for s in range(SLOTS[kind]):
                    if 1 <= s <= NTILES[kind]:
                        normalise(kind, tau, s - 1)
                    if more:
                        project(kind, pair + 1, tau, s)
                out_low(kind, pair)

            def out_low(kind, pair):
                pool.wait_ge(o_hi_done, pair + 1)
                k = pair - 8 if kind == "c" else pair
                dst, hi = o_lo[:, bass.ds(k, 1), :], o_hi[:, bass.ds(k, 1), :]
                tt(dst, of[:].rearrange("p (k s) -> p k s", k=1), hi.bitcast(F32), sub).then_inc(o_lo_done, 1)

            def pairs(kind, pair0, n, tau0):
                if kind != "c":
                    for s in range(SLOTS[kind]):
                        project(kind, pair0, 0, s)
                else:
                    pool.wait_ge(cmask_landed, 16)
                    pool.wait_ge(bias_landed, 16)
                    biases(pair0, 0)
                    biases(pair0, 1)
                with pool.Fori(0, n - 1) as i:
                    heads(kind, i + pair0, i * NTILES[kind] + tau0, True)
                heads(kind, pair0 + n - 1, tau0 + (n - 1) * NTILES[kind], False)

            def columns(sq0):
                with pool.Fori(0, 8) as m:
                    square_add(m + sq0)

            def ffn(layer):
                with pool.Fori(0, FT) as f:
                    pool.wait_ge(hid_hi_done, f + (layer * FT + 1))
                    tt(h_lo[:, bass.ds(f, 1), :], rk[:].rearrange("p (k s) -> p k s", k=1),
                       h_hi[:, bass.ds(f, 1), :].bitcast(F32), sub).then_inc(hid_lo_done, 1)
                columns(END["f0" if layer == 0 else "f1"])

            pool.sem_inc(o_lo_done, CR_OLO)
            nc.gpsimd.memset(acc[:], 0.0).then_inc(acc_zero, 1)
            pool.wait_ge(acc_zero, 1)
            for k in range(KT):
                square_add(k)
            clear(0)
            norm_low(0)
            square_add(8)
            square_add(9)
            clear(1)
            square_add(10)
            norm_low(1)
            clear(2)
            norm_low(2)
            pool.wait_ge(tabB_landed, 16)
            pairs("a", 0, A_PAIRS, 0)
            pairs("b", A_PAIRS, B_PAIRS, 8 * A_PAIRS)
            columns(END["kv"])
            clear(3)
            norm_low(3)
            pool.dma_start(cm, cmask).then_inc(cmask_landed, 16)
            load_biases(8)
            ffn(0)
            clear(4)
            norm_low(4)
            pairs("c", 8, C_PAIRS, 8 * (A_PAIRS + B_PAIRS))
            columns(END["od"])
            clear(5)
            norm_low(5)
            ffn(1)
            clear(6)


def _rows(w, cols):
    import numpy as np
    a = np.ascontiguousarray(w[:, cols]) if not isinstance(cols, slice) else w[:, cols]
    if a.shape[1] < P:
        a = np.concatenate([a, np.zeros((a.shape[0], P - a.shape[1]), a.dtype)], axis=1)
    return [a[k * P:(k + 1) * P] for k in range(a.shape[0] // P)]


def _chunks(tiles, per):
    import numpy as np
    zero = np.zeros((P, P), np.float32)
    tiles = [zero if t is None else t for t in tiles]
    a = np.stack(tiles).reshape(len(tiles) // per, per, P, P)
    return np.ascontiguousarray(a.transpose(0, 2, 1, 3).reshape(len(tiles) // per, P, per * P))


def _layout(i):
    import numpy as np
    ar = np.arange
    nat = (ar(S) % 8) * 64 + ar(S) // 8
    w_in, q_up, kv_up = i["ev_w_in"][0], i["ev_w_q_up"][0], i["ev_w_kv_up"][0]
    swap = np.r_[16:32, 0:16]
    t = {}
    kpe = QR + KVR + ar(ROPE)
    t["a0"] = sum([_rows(w_in, ar(m * P, m * P + P)) for m in range(3)], []) + _rows(w_in, np.r_[kpe, kpe[swap]])
    t["a"], t["b"] = [], []
    for pr in range(A_PAIRS):
        for h in (2 * pr, 2 * pr + 1):
            c = h * QA
            t["a"] += _rows(q_up, np.r_[c + ar(QA), c + NOPE + swap])
        c0, c1 = 4 * pr * 64, (4 * pr + 2) * 64
        t["a"] += _rows(kv_up, np.r_[c0 + 64 + ar(64), c1 + 64 + ar(64)]) + [None]
        t["a"] += _rows(kv_up, np.r_[c0 + ar(64), c1 + ar(64)]) + [None]
        for m in range(3):
            t["b"] += _rows(w_in, 416 + 512 * m + 128 * pr + ar(P))
    t["eo"] = sum([_rows(i["ev_w_out"][0], m * P + ar(P)) for m in range(8)], [])
    t["oo"] = sum([_rows(i["od_w_out"][0], m * P + ar(P)) for m in range(8)], [])
    t["c"] = sum([_rows(i["od_w_qkv"][0], m * DM + pr * P + ar(P)) for pr in range(8) for m in range(3)], [])
    for l in range(2):
        t[f"u{l}"] = sum([_rows(i[w][l], f * P + ar(P)) for f in range(FT) for w in ("ffn_w_gate", "ffn_w_up")], [])
        t[f"d{l}"] = sum([_rows(i["ffn_w_down"][l], m * P + ar(P)) + [None, None] for m in range(8)], [])
    arrays = {f"w_{k}": _chunks(v, PER[k]) for k, v in t.items()}
    arrays["xT"] = np.ascontiguousarray(i["x"][0][nat].T.reshape(KT, P, S).transpose(1, 0, 2))
    g = np.zeros((P, 48), np.float32)
    for name, a in (("ev", i["ev_norm"][0]), ("f0", i["ffn_norm"][0]), ("od", i["od_norm"][0]),
                    ("f1", i["ffn_norm"][1]), ("fin", i["final_norm"]), ("q", i["ev_q_norm"][0]),
                    ("kv", i["ev_kv_norm"][0])):
        a = a.reshape(-1, P).T
        g[:, GAIN[name]:GAIN[name] + a.shape[1]] = a
    arrays["gains"] = g
    arrays["consts"] = np.stack([np.eye(P, dtype=np.float32), np.ones((P, P), np.float32)], axis=1)

    def rope(dim):
        inv = np.float32(10000.0) ** (-np.arange(0, dim, 2, dtype=np.float32) / np.float32(dim))
        ang = nat.astype(np.float32)[None, :] * inv.astype(np.float32)[:, None]
        return np.cos(ang), np.sin(ang)

    ca, sa = rope(ROPE)
    cb, sbn = rope(HD)
    scale = float(QA) ** -0.5
    a = np.zeros((P, 2, S), np.float32)
    a[0:NOPE, 0] = -scale
    a[NOPE:QA, 0] = -scale * np.r_[ca, ca]
    a[QA:, 0] = np.r_[-sa, sa]
    a[0:ROPE, 1] = np.r_[ca, ca]
    a[NOPE:QA, 1] = -scale * np.r_[-sa, sa]
    arrays["tabA"] = a
    C, R = np.tile(np.r_[cb, cb], (2, 1)), np.tile(np.r_[-sbn, sbn], (2, 1))
    arrays["tabB"] = np.ascontiguousarray(np.stack([-0.125 * C, -0.125 * R, C, R], axis=1).astype(np.float32))
    d = np.abs(nat[:, None] - nat[None, :])
    count = sum(((d % dil == 0) & (d // dil <= win // (2 * dil))).astype(np.float32)
                for win, dil in ((128, 1), (512, 4), (2048, 16)))
    lnc = np.where(count > 0, -np.log(np.maximum(count, 1)), 1e30).astype(np.float32)
    arrays["lnc"] = np.ascontiguousarray(lnc.reshape(4, P, S).transpose(1, 0, 2))
    cm = np.zeros((P, 3, BAND), np.float32)
    for kind, j in enumerate((0, 1, 3)):
        qc = 16 * j + np.arange(P) // 8
        kc = BAND_START[j] // 8 + np.arange(BAND) // 8
        start = np.clip(qc - 8, 0, 48)[:, None]
        cm[:, kind] = np.where((kc[None] >= start) & (kc[None] < start + 16), 0.0, 1e30)
    arrays["cmask"] = cm
    rpb = i["od_rpb"][0]
    pad = np.zeros((16, 15, 31 + 17 + 17), np.float32)
    pad[:, :, 17:48] = rpb
    wide = np.zeros((16, P, 48, 8), np.float32)
    for q in range(P):
        qc, r = q // 8, q % 8
        wide[:, q] = pad[:, 7 - r:15 - r, 16 - qc:64 - qc].transpose(0, 2, 1)
    arrays["bias"] = wide.reshape(16, P, WIDE)
    return arrays, nat


def kernel(**inputs):
    import numpy as np
    import concourse.bacc as bacc
    from concourse.bass_utils import run_bass_kernel_spmd

    arrays, nat = _layout({k: np.asarray(v) for k, v in inputs.items()})
    nc = bacc.Bacc("TRN2", target_bir_lowering=False, num_devices=1)
    ap = {k: nc.dram_tensor(f"in_{k}", v.shape, mybir.dt.from_np(v.dtype), kind="ExternalInput").ap()
          for k, v in arrays.items()}
    out = nc.dram_tensor("out_y", (P, KT, S), F32, kind="ExternalOutput").ap()
    build(nc, ap["xT"], ap["gains"], ap["consts"], ap["tabA"], ap["tabB"], ap["lnc"], ap["cmask"], ap["bias"],
          {k: ap[f"w_{k}"] for k in STREAM}, out)
    r = run_bass_kernel_spmd(nc, [{f"in_{k}": v for k, v in arrays.items()}], core_ids=[0])
    y = r.results[0]["out_y"].transpose(1, 0, 2).reshape(DM, S).T
    back = np.empty_like(y)
    back[nat] = y
    return back[None]
```

```python
from contextlib import ExitStack

import concourse.bass as bass
from concourse import mybir

F32 = mybir.dt.float32
F32R = mybir.dt.float32r
ALU = mybir.AluOpType
ACT = mybir.ActivationFunctionType
AX = mybir.AxisListType.X

P = 128
S = 512
DM = 1024
KT = DM // P
HD = 64
NOPE, ROPE = 64, 32
QA = NOPE + ROPE
QR, KVR = 256, 128
DFF = 2816
FT = DFF // P
A_PAIRS = B_PAIRS = 4
C_PAIRS = 8
RING = 4
EPS = 1e-6

STREAM = {
    "a0": (4, 8, 1, 32),
    "a": (2, 16, A_PAIRS, 6),
    "b": (3, 32, B_PAIRS, 24),
    "eo": (4, 16, 4, 16),
    "u0": (4, 4 * FT, FT, 16),
    "d0": (3, 64, 4, 2 * FT),
    "c": (3, 64, C_PAIRS, 24),
    "oo": (4, 16, 4, 16),
    "u1": (4, 4 * FT, FT, 16),
    "d1": (3, 64, 4, 2 * FT),
}
PER = {k: v[0] for k, v in STREAM.items()}
STEP_CHUNKS = {k: v[1] // v[2] for k, v in STREAM.items()}
STEP_TILES = {k: v[3] for k, v in STREAM.items()}
CHUNK0, TILE0 = {}, {}
_c = _t = 0
for _k, (_per, _n, _steps, _tiles) in STREAM.items():
    CHUNK0[_k], TILE0[_k] = _c, _t
    _c, _t = _c + _n, _t + _steps * _tiles


def through(phase, k):
    if phase == "a":
        return [2, 4, 5, 6][k]
    if phase in ("d0", "d1"):
        return (k // 8) * FT + min(3 * (k % 8 + 1), FT)
    return PER[phase] * (k + 1)


USED = [TILE0[ph] + st * STEP_TILES[ph] + through(ph, k)
        for ph, v in STREAM.items() for st in range(v[2]) for k in range(STEP_CHUNKS[ph])]

GAIN = {"ev": 0, "f0": 8, "od": 16, "f1": 24, "fin": 32, "q": 40, "kv": 42}
BAND_START = [0, 64, 192, 256]
BAND_KIND = [0, 1, 1, 2]
WIDE_OFF = [128, 64, 0]
BAND = 256
WIDE = 384


def build(nc, xT, gains, consts, tabA, tabB, lnc, cmask, bias, streams, out):
    ctx = ExitStack()
    with ctx:
        def sb(name, shape, dt=F32):
            return ctx.enter_context(nc.sbuf_tensor(name, shape, dt))

        def sem(name):
            return ctx.enter_context(nc.semaphore(name))

        x = sb("x_res", [P, KT, S])
        xn_hi = sb("xn_hi", [P, KT, S], F32R)
        xn_lo = sb("xn_lo", [P, KT, S], F32R)
        w_raw = sb("w_raw", [P, RING, 4 * P])
        w_hi = sb("w_hi", [P, RING, 4 * P], F32R)
        w_lo = sb("w_lo", [P, RING, 4 * P], F32R)
        shared = sb("shared", [P, 2 * FT * S], F32R)
        gain = sb("gain", [P, 48])
        cst = sb("cst", [P, 2, P])
        tabs = sb("tabs", [P, 10 * S])
        p = sb("p", [P, 4, S])
        rq = sb("rq", [P, S])
        rk = sb("rk", [P, S])
        sw = sb("sw", [P, S])
        vT = sb("vT", [P, S])
        to = sb("to", [P, S])
        of = sb("of", [P, S])
        acc = sb("acc", [P, S])
        small = sb("small", [P, 64])
        ps = ctx.enter_context(nc.psum_tensor("ps", [P, 8, S], F32))

        ident, ones = cst[:, 0, :], cst[:, 1, :]
        PJ, SC, PTB, OB = 0, 3, 5, 7
        mn, den, rden = small[:, 0:16], small[:, 16:32], small[:, 32:48]
        mean, root, rinv = small[:, 48:52], small[:, 52:56], small[:, 56:60]

        def part(off, n):
            return shared[:, off:off + n]

        q_hi = part(0, 2 * S).rearrange("p (h s) -> p h s", h=2)
        q_lo = part(2 * S, 2 * S).rearrange("p (h s) -> p h s", h=2)
        k_hi = part(4 * S, 2 * S).rearrange("p (h s) -> p h s", h=2)
        k_lo = part(6 * S, 2 * S).rearrange("p (h s) -> p h s", h=2)
        v_st = part(8 * S, 2 * S).rearrange("p (t h e d) -> p t h e d", t=4, h=2, e=2)
        pt_hi = part(10 * S, 4 * S)
        pt_lo = part(14 * S, 4 * S)
        cn_hi = part(18 * S, 3 * S).rearrange("p (k s) -> p k s", k=3)
        cn_lo = part(21 * S, 3 * S).rearrange("p (k s) -> p k s", k=3)
        v_sh = part(18 * S, 3 * S // 2).rearrange("p (t h e d) -> p t h e d", t=3, h=2, e=2)
        o_hi = part(24 * S, 8 * S).rearrange("p (k s) -> p k s", k=8)
        o_lo = part(32 * S, 8 * S).rearrange("p (k s) -> p k s", k=8)
        h_hi = part(0, FT * S).rearrange("p (k s) -> p k s", k=FT)
        h_lo = part(FT * S, FT * S).rearrange("p (k s) -> p k s", k=FT)

        tA = tabs[:, 0:2 * S].rearrange("p (k s) -> p k s", k=2)
        tB = tabs[:, 2 * S:6 * S].rearrange("p (k s) -> p k s", k=4)
        tM = tabs[:, 6 * S:10 * S].rearrange("p (k s) -> p k s", k=4)
        wide = tabs[:, 0:2 * WIDE].rearrange("p (h w) -> p h w", h=2)
        cm = tabs[:, 2 * WIDE:2 * WIDE + 3 * BAND].rearrange("p (k w) -> p k w", k=3)
        bt = tabs[:, 1536:1536 + 6 * BAND].rearrange("p (h k w) -> p h k w", h=2, k=3)

        landed = [sem(f"landed{s}") for s in range(RING)]
        x_landed, gain_landed, cst_landed, tabA_landed, tabB_landed, lnc_landed, cmask_landed, bias_landed, \
            vsh_landed, vsh2_landed = [sem(n) for n in (
                "x_landed gain_landed cst_landed tabA_landed tabB_landed lnc_landed cmask_landed bias_landed "
                "vsh_landed vsh2_landed").split()]
        tile_used, ss_done, rbc_done, score_done, pt_done, vt_done, pv_done = [sem(n) for n in (
            "tile_used ss_done rbc_done score_done pt_done vt_done pv_done").split()]
        w_hi_ready, square_done, root_done, xn_hi_done, exp_done, pt_hi_done, vT_done, v_hi_done, o1_done, \
            o_hi_done, c_done, swap_done, stage_hi_done, silu_done, hid_hi_done = [sem(n) for n in (
                "w_hi_ready square_done root_done xn_hi_done exp_done pt_hi_done vT_done v_hi_done o1_done "
                "o_hi_done c_done swap_done stage_hi_done silu_done hid_hi_done").split()]
        w_lo_ready, mean_done, diag_done, rinv_done, xf_done, min_done, rden_done, pt_lo_done, v_lo_done, o2_done, \
            rope_t_done, staged, kpe_done, pads_done, hid_done, res_done, fin_done, minima_go = [sem(n) for n in (
                "w_lo_ready mean_done diag_done rinv_done xf_done min_done rden_done pt_lo_done v_lo_done o2_done "
                "rope_t_done staged kpe_done pads_done hid_done res_done fin_done minima_go").split()]
        acc_zero, acc_done, xn_done, norm_done, rope_m_done, rope_done, o_lo_done, bias_ready, hid_lo_done = [
            sem(n) for n in (
                "acc_zero acc_done xn_done norm_done rope_m_done rope_done o_lo_done bias_ready hid_lo_done").split()]
        stored = sem("stored")

        CR_EXP, CR_PT, CR_PV, CR_PTL, CR_OLO, CR_SILU, CR_HID, CR_RES = 2, 4, 2, 2, 1, 1, 1, 2

        NORMS = ["ev", "q", "kv", "f0", "od", "f1", "fin"]
        WIDTH = {"ev": 8, "q": 2, "kv": 1, "f0": 8, "od": 8, "f1": 8, "fin": 8}
        END = {}
        n_tiles = 0
        for name in NORMS:
            n_tiles += WIDTH[name]
            END[name] = n_tiles

        def norm_src(name):
            if name == "q":
                return [rq[:], rk[:]]
            if name == "kv":
                return [vT[:]]
            return [x[:, k, :] for k in range(KT)]

        def norm_dst(name):
            if name == "q":
                return [(cn_hi[:, k, :], cn_lo[:, k, :]) for k in (0, 1)]
            if name == "kv":
                return [(cn_hi[:, 2, :], cn_lo[:, 2, :])]
            return [(xn_hi[:, k, :], xn_lo[:, k, :]) for k in range(KT)]

        SLOTS, SPAN = 8, 15
        NTILES = {"a": 8, "b": 8, "c": 4}
        GAP = {"a": 1, "b": 1, "c": 2}
        PAIR0 = {"a": 0, "b": A_PAIRS, "c": 8}
        PV = {"a": {6: 0, 8: 1, 10: 2, 12: 3}, "c": {7: 0, 11: 1}}
        OUT = {"a": {9: 0, 13: 1}, "c": {8: 0, 12: 1}}
        OUT_SPLIT = {"a": 14, "c": 13}
        VALUES = {"a": {2: 0, 5: 1}, "c": {2: 0, 4: 1}}
        for config in (PV, OUT, OUT_SPLIT, VALUES):
            config["b"] = config["a"]
        SPLITS = {"a": {0: [0], 1: [1], 3: [2], 4: [3]}, "b": {0: [0, 1], 1: [2, 3], 2: [4], 3: [5], 5: [6], 6: [7]},
                  "c": {0: [0, 1], 1: [2], 2: [3], 3: [4], 4: [5], 5: [6], 6: [7]}}
        FILL = {"b": [2, 4, 4, 4, 2, 0, 4, 4], "c": [3] * 8}

        def tile_at(kind, j, lag):
            t, r = divmod(j - lag, GAP[kind])
            return t if r == 0 and 0 <= t < NTILES[kind] else None

        def tau(kind, pair):
            return pair * 4 + 32 if kind == "c" else pair * 8

        def outputs_ahead(kind, pair):
            return pair * 2 + 16 if kind == "c" else pair * 4

        block = ctx.enter_context(nc.Block())

        @block.sync
        def _(sp):
            for h in range(2):
                sp.dma_start(x[:, 4 * h:4 * h + 4, :], xT[:, 4 * h:4 * h + 4, :]).then_inc(x_landed, 16)
            sp.dma_start(gain[:], gains).then_inc(gain_landed, 16)
            sp.dma_start(cst[:], consts).then_inc(cst_landed, 16)
            for name in STREAM:
                per, n = STREAM[name][0:2]
                base, src = CHUNK0[name], streams[name]
                if name == "a0":
                    for c in range(n):
                        if c >= RING:
                            sp.wait_ge(w_lo_ready, c - RING + 1)
                        sp.dma_start(w_raw[:, c % RING, 0:per * P], src[c]).then_inc(landed[c % RING], 16)
                        if c == 3:
                            sp.dma_start(tA, tabA).then_inc(tabA_landed, 16)
                            sp.dma_start(tB, tabB).then_inc(tabB_landed, 16)
                            sp.dma_start(tM, lnc).then_inc(lnc_landed, 16)
                    continue
                with sp.Fori(0, n // RING) as i:
                    for s in range(RING):
                        sp.wait_ge(w_lo_ready, i * RING + (base + s - RING + 1))
                        sp.dma_start(w_raw[:, s, 0:per * P],
                                     src[bass.ds(i * RING + s, 1)].rearrange("c p w -> p (c w)")
                                     ).then_inc(landed[s], 16)
            for k in range(KT):
                sp.wait_ge(fin_done, k + 1)
                sp.dma_start(out[:, k, :], x[:, k, :]).then_inc(stored, 16)
            sp.wait_ge(stored, 16 * KT)

        @block.tensor
        def _(pe):
            mm = nc.tensor.matmul

            def weight_tile(phase, c0, n, bank, rhs, first, final, cols=P):
                per = PER[phase]
                if n % per == 0:
                    pe.wait_ge(w_lo_ready, c0 + (n // per + 1))
                s, o = (n // per) % RING, (n % per) * P
                a, b = w_hi[:, s, o:o + cols], w_lo[:, s, o:o + cols]
                r_hi, r_lo = rhs
                dst = ps[0:cols, bank, :]
                mm(dst, a, r_hi, start=first, stop=False)
                mm(dst, a, r_lo, start=False, stop=False)
                mm(dst, b, r_hi, start=False, stop=final).then_inc(tile_used, 1)

            def norm(n):
                name = NORMS[n]
                pe.wait_ge(acc_done, END[name])
                for t in range(4):
                    last = mm(ps[:, SC, t:t + 1], acc[:, t * P:(t + 1) * P], ones[:, 0:1], start=True, stop=True)
                last.then_inc(ss_done, 1)
                pe.wait_ge(diag_done, n + 1)
                for t in range(4):
                    last = mm(ps[:, SC + 1, t * P:(t + 1) * P], ones, of[:, t * P:(t + 1) * P],
                              start=True, stop=True)
                last.then_inc(rbc_done, 1)

            def xn(k):
                return xn_hi[:, k, :], xn_lo[:, k, :]

            def cn(k):
                return cn_hi[:, k, :], cn_lo[:, k, :]

            def values(pair):
                pe.wait_ge(vT_done, pair + 1)
                if not isinstance(pair, int) or pair > 0:
                    pe.wait_ge(v_lo_done, pair * 2)
                for t in range(4):
                    last = nc.tensor.transpose(ps[:, PJ + 2, t * P:(t + 1) * P], vT[:, t * P:(t + 1) * P], ident)
                last.then_inc(vt_done, 1)

            def scores(kind, pair, t):
                half = NTILES[kind] // 2
                if t % half == 0:
                    pe.wait_ge(staged, pair * 2 + (t // half + 1))
                if kind == "a" or (t < 2 and isinstance(pair, int) and pair == A_PAIRS):
                    pe.wait_ge(exp_done, tau(kind, pair) + (t + CR_EXP - 1))
                if kind == "a":
                    rows, h, kh = QA, t // 4, t // 4
                else:
                    pe.wait_ge(min_done, tau(kind, pair) + (t - 1))
                    rows, h, kh = P, t // (NTILES[kind] // 2), 0
                o = ps[:, SC + t % 2, :]
                if kind == "c":
                    for u in range(2):
                        j = 2 * (t % 2) + u
                        ou = o[:, u * BAND:(u + 1) * BAND]
                        qs, ks = slice(j * P, (j + 1) * P), slice(BAND_START[j], BAND_START[j] + BAND)
                        mm(ou, q_hi[:, h, qs], k_hi[:, 0, ks], start=True, stop=False)
                        mm(ou, q_hi[:, h, qs], k_lo[:, 0, ks], start=False, stop=False)
                        last = mm(ou, q_lo[:, h, qs], k_hi[:, 0, ks], start=False, stop=True)
                else:
                    qs = slice((t % 4) * P, (t % 4 + 1) * P)
                    mm(o, q_hi[0:rows, h, qs], k_hi[0:rows, kh, :], start=True, stop=False)
                    mm(o, q_hi[0:rows, h, qs], k_lo[0:rows, kh, :], start=False, stop=False)
                    last = mm(o, q_lo[0:rows, h, qs], k_hi[0:rows, kh, :], start=False, stop=True)
                last.then_inc(score_done, 1)

            def turn(kind, pair, t):
                pe.wait_ge(norm_done, tau(kind, pair) + (t + 1))
                pe.wait_ge(pt_lo_done, tau(kind, pair) + (t + CR_PTL - 1))
                for kt in range(4):
                    last = nc.tensor.transpose(ps[:, PTB + t % 2, kt * P:(kt + 1) * P],
                                               p[:, t % 4, kt * P:(kt + 1) * P], ident)
                last.then_inc(pt_done, 1)

            def outputs(kind, pair, u):
                h, tiles, first = (u, 2 * u + 2, True) if kind == "c" else (u // 2, 2 * u + 2, u % 2 == 0)
                pe.wait_ge(pt_lo_done, tau(kind, pair) + (tiles + CR_PTL))
                if first:
                    pe.wait_ge(o2_done, pair * 2 + (h + 1))
                    pe.wait_ge(v_lo_done, pair * 2 + (h + 1))
                if kind == "c":
                    if h == 0:
                        pe.wait_ge(vsh_landed, (pair - 7) * 16)
                        pe.wait_ge(vsh2_landed, (pair - 7) * 16)
                    for j in range(4):
                        o = ps[:, OB, j * P:(j + 1) * P]
                        for kt in range(2):
                            v = v_st[:, (j // 3) * 2 + kt, h] if j in (0, 3) else v_sh[:, j - 1 + kt, h]
                            v = v.rearrange("p e d -> p (e d)")
                            c = h * 2 * S + (j * 2 + kt) * P
                            mm(o, v, pt_hi[:, c:c + P], start=(kt == 0), stop=False)
                            last = mm(o, v, pt_lo[:, c:c + P], start=False, stop=(kt == 1))
                else:
                    q0 = (u % 2) * 2 * P
                    for kt in range(4):
                        v = v_st[:, kt, h].rearrange("p e d -> p (e d)")
                        o, qs = ps[:, OB, q0:q0 + 2 * P], slice(kt * S + q0, kt * S + q0 + 2 * P)
                        mm(o, v, pt_hi[:, qs], start=(kt == 0), stop=False)
                        last = mm(o, v, pt_lo[:, qs], start=False, stop=(kt == 3))
                last.then_inc(pv_done, 1)

            def project(kind, pair, s):
                step = pair - PAIR0[kind]
                c0 = step * STEP_CHUNKS[kind] + CHUNK0[kind]
                later = not isinstance(pair, int) or pair > 0
                if kind == "a":
                    if s == 1:
                        if later:
                            pe.wait_ge(vT_done, pair)
                        for k in range(2):
                            weight_tile("a", c0, k, PJ, cn(k), k == 0, k == 1)
                    elif s == 2:
                        if later:
                            pe.wait_ge(staged, pair * 2)
                        for k in range(2):
                            weight_tile("a", c0, 2 + k, PJ + 1, cn(k), k == 0, k == 1)
                    elif s == 4:
                        pe.wait_ge(rope_t_done, pair * 2 + 1)
                        weight_tile("a", c0, 4, PJ, cn(2), True, True)
                    elif s == 5:
                        pe.wait_ge(rope_t_done, pair * 2 + 2)
                        weight_tile("a", c0, 6, PJ + 1, cn(2), True, True)
                    return
                m0 = sum(FILL[kind][:s])
                for m in range(m0, m0 + FILL[kind][s]):
                    if m == 0 and isinstance(pair, int) and pair == A_PAIRS:
                        pe.wait_ge(vT_done, pair)
                    if m == 8:
                        pe.wait_ge(staged, pair * 2)
                    if m == 16:
                        pe.wait_ge(v_lo_done, pair * 2)
                    weight_tile(kind, c0, m, PJ + m // KT, xn(m % KT), m % KT == 0, m % KT == KT - 1)

            def work(kind, pair, j):
                t = tile_at(kind, j, 0)
                if t is not None:
                    scores(kind, pair, t)
                t = tile_at(kind, j, 3)
                if t is not None:
                    turn(kind, pair, t)
                if j in PV[kind]:
                    outputs(kind, pair, PV[kind][j])
                if j == 1:
                    values(pair)

            def heads(before, kind, pair, after):
                for s in range(SLOTS):
                    if before:
                        work(before, pair - 1, s + SLOTS)
                    work(kind, pair, s)
                    if after:
                        project(after, pair + 1, s)

            def pairs(kind, n, before, after):
                p0 = PAIR0[kind]
                if before is None:
                    for s in range(SLOTS):
                        project(kind, p0, s)
                heads(before, kind, p0, kind)
                with pe.Fori(p0 + 1, p0 + n - 1) as pair:
                    heads(kind, kind, pair, kind)
                heads(kind, kind, p0 + n - 1, after)
                if after is None:
                    for j in range(SLOTS, SPAN):
                        work(kind, p0 + n - 1, j)

            def columns(phase, m0, nk, rhs):
                with pe.Fori(0, 4) as i:
                    for u in range(2):
                        pe.wait_ge(res_done, i * 2 + (m0 + u + 1))
                        for k in range(nk):
                            n = u * PER[phase] * STEP_CHUNKS[phase] // 2 + k
                            weight_tile(phase, i * STEP_CHUNKS[phase] + CHUNK0[phase], n, PTB + u, rhs(k), k == 0,
                                        k == nk - 1)

            def ffn(layer):
                phase = f"u{layer}"
                with pe.Fori(0, FT) as f:
                    for g in range(2):
                        free = (silu_done, CR_SILU) if g == 0 else (hid_done, CR_HID)
                        pe.wait_ge(free[0], f + (layer * FT + free[1]))
                        for k in range(KT):
                            weight_tile(phase, f * 4 + CHUNK0[phase], g * KT + k, g, xn(k), k == 0, k == KT - 1)
                pe.wait_ge(hid_lo_done, (layer + 1) * FT)
                columns(f"d{layer}", 8 + 16 * layer, FT, lambda k: (h_hi[:, k, :], h_lo[:, k, :]))

            pe.sem_inc(pt_done, CR_PT)
            pe.sem_inc(pv_done, CR_PV)
            pe.wait_ge(cst_landed, 16)
            norm(0)
            for m in range(4):
                for k in range(KT):
                    if m == 0:
                        pe.wait_ge(xn_done, k + 1)
                    weight_tile("a0", 0, m * KT + k, (PJ, PJ + 1, PJ + 2, OB)[m], xn(k), k == 0, k == KT - 1,
                                cols=P if m < 3 else 2 * ROPE)
            norm(1)
            norm(2)
            pe.wait_ge(xn_done, END["kv"])
            pairs("a", A_PAIRS, None, "b")
            pairs("b", B_PAIRS, "a", None)
            pe.wait_ge(o_lo_done, 8 + CR_OLO)
            columns("eo", 0, KT, lambda k: (o_hi[:, k, :], o_lo[:, k, :]))
            norm(3)
            pe.wait_ge(xn_done, END["f0"])
            ffn(0)
            norm(4)
            pe.wait_ge(xn_done, END["od"])
            pairs("c", C_PAIRS, None, None)
            pe.wait_ge(o_lo_done, 16 + CR_OLO)
            columns("oo", 16, KT, lambda k: (o_hi[:, k, :], o_lo[:, k, :]))
            norm(5)
            pe.wait_ge(xn_done, END["f1"])
            ffn(1)
            norm(6)

        @block.scalar
        def _(act):
            def copy(out, in_, scale=1.0):
                return nc.scalar.activation(out, in_, ACT.Copy, scale=scale)

            def split(phase, step, k):
                per, w = PER[phase], PER[phase] * P
                c = step * STEP_CHUNKS[phase] + (CHUNK0[phase] + k)
                act.wait_ge(landed[k % RING], chunk_bytes(phase, step, k))
                if isinstance(step, int):
                    if c >= RING:
                        act.wait_ge(tile_used, USED[c - RING])
                else:
                    K = STEP_CHUNKS[phase]
                    j = k - RING
                    back = through(phase, j) if j >= 0 else through(phase, j + K) - STEP_TILES[phase]
                    act.wait_ge(tile_used, step * STEP_TILES[phase] + (TILE0[phase] + back))
                copy(w_hi[:, k % RING, 0:w], w_raw[:, k % RING, 0:w]).then_inc(w_hi_ready, 1)

            def chunk_bytes(phase, step, k):
                K = STEP_CHUNKS[phase]
                return step * (16 * K // RING) + 16 * ((CHUNK0[phase] + k) // RING + 1)

            def square(src, n):
                if n >= 1:
                    act.wait_ge(acc_done, n)
                nc.scalar.activation(sw[:], src, ACT.Square).then_inc(square_done, 1)

            def norm(n):
                name = NORMS[n]
                act.wait_ge(mean_done, n + 1)
                nc.scalar.activation(root, mean, ACT.Sqrt).then_inc(root_done, 1)
                if name == "fin":
                    return
                g0 = END[name] - WIDTH[name]
                for k, (hi, lo) in enumerate(norm_dst(name)):
                    act.wait_ge(xf_done, g0 + k + 1)
                    copy(hi, p[:, (g0 + k) % 4, :]).then_inc(xn_hi_done, 1)

            def exps(kind, pair, t):
                act.wait_ge(min_done, tau(kind, pair) + (t + 1))
                if kind == "a":
                    act.wait_ge(pt_done, tau(kind, pair) + (t + 1))
                    nc.scalar.activation(p[:, t % 4, :], ps[:, SC + t % 2, :], ACT.Exp, bias=mn[:, t:t + 1], scale=-1.0,
                                         accum_out=den[:, t:t + 1]).then_inc(exp_done, 1)
                    return
                n = 2 if kind == "c" else 1
                w = S // n
                for u in range(n):
                    c = n * t + u
                    pu = p[:, t % 4, u * w:(u + 1) * w]
                    last = nc.scalar.activation(pu, pu, ACT.Exp, bias=mn[:, c:c + 1], scale=-1.0,
                                                accum_out=den[:, c:c + 1])
                last.then_inc(exp_done, 1)

            def turned(kind, pair, t):
                act.wait_ge(pt_done, tau(kind, pair) + (t + 1 + CR_PT))
                if t % 2 == 0:
                    act.wait_ge(pv_done, outputs_ahead(kind, pair) + (t // 2 + 1))
                src = ps[:, PTB + t % 2, :]
                if kind == "c":
                    copy(pt_hi[:, t * S:(t + 1) * S], src).then_inc(pt_hi_done, 1)
                else:
                    dst = pt_hi.rearrange("p (k s) -> p k s", k=4)[:, :, (t % 4) * P:(t % 4 + 1) * P]
                    copy(dst, src.rearrange("p (k s) -> p k s", k=4)).then_inc(pt_hi_done, 1)

            def out_low(kind, pair, h):
                n = h + 1 if kind == "c" else 2 * h + 2
                act.wait_ge(pv_done, outputs_ahead(kind, pair) + (n + CR_PV))
                copy(to[h * HD:(h + 1) * HD, :], ps[HD:P, OB, :]).then_inc(o1_done, 1)

            def out_high(kind, pair):
                act.wait_ge(o2_done, pair * 2 + 3)
                k = pair - 8 if kind == "c" else pair
                copy(o_hi[:, bass.ds(k, 1), :], of[:].rearrange("p (k s) -> p k s", k=1)).then_inc(o_hi_done, 1)

            def values_high(kind, pair, h):
                if h == 0:
                    act.wait_ge(vt_done, pair + 1)
                else:
                    act.wait_ge(v_lo_done, pair * 2 + 1)
                if kind == "c":
                    act.wait_ge(pv_done, outputs_ahead(kind, pair) + (h + 1))
                elif not isinstance(pair, int) or pair > 0:
                    act.wait_ge(pv_done, outputs_ahead(kind, pair) + 2 * h)
                src = ps[:, PJ + 2, :].rearrange("p (t h d) -> p t h d", t=4, h=2)
                copy(v_st[:, :, h, 0, :], src[:, :, h, :]).then_inc(v_hi_done, 1)

            def shift_values(pair):
                act.wait_ge(v_lo_done, pair * 2 + 2)
                flat = v_st.rearrange("p t h e d -> p t (h e d)")
                dst = v_sh.rearrange("p t h e d -> p t (h e d)")
                act.dma_start(dst[0:HD].bitcast(F32), flat[HD:P, 0:3].bitcast(F32)).then_inc(vsh_landed, 16)
                act.dma_start(dst[HD:P].bitcast(F32), flat[0:HD, 1:4].bitcast(F32)).then_inc(vsh2_landed, 16)

            def project(kind, pair, s):
                step = pair - PAIR0[kind]

                def tiles(n):
                    act.wait_ge(tile_used, step * STEP_TILES[kind] + (TILE0[kind] + n))

                def scores_used(n):
                    if not (isinstance(pair, int) and pair in (0, 8)):
                        act.wait_ge(score_done, tau(kind, pair) + (n - NTILES[kind]))

                if kind == "a":
                    if s == 5:
                        tiles(5)
                        copy(vT[:], ps[:, PJ, :]).then_inc(vT_done, 1)
                    if s in (6, 8):
                        h = 0 if s == 6 else 1
                        scores_used(4 * (h + 1))
                        act.wait_ge(rope_done, pair * 2 + (h + 1))
                        copy(q_hi[0:QA, h, :], (rq, rk)[h][0:QA, :])
                        tiles(6)
                        copy(k_hi[0:NOPE, h, :], ps[h * NOPE:(h + 1) * NOPE, PJ + 1, :]).then_inc(stage_hi_done, 1)
                    return
                if s == 8:
                    tiles(24)
                    copy(vT[:], ps[:, PJ + 2, :]).then_inc(vT_done, 1)
                if kind == "b":
                    if s in (3, 5):
                        m = 0 if s == 3 else 1
                        tiles(8 * (m + 1))
                        act.wait_ge(rope_done, pair * 2 + m)
                        act.wait_ge(rope_t_done, pair * 2 + (m + 1))
                        for g in range(4):
                            last = copy(sw[32 * g:32 * g + 32, :], ps[32 * (g ^ 1):32 * (g ^ 1) + 32, PJ + m, :])
                        last.then_inc(swap_done, 1)
                    if s == 7:
                        scores_used(8)
                        act.wait_ge(rope_done, pair * 2 + 2)
                        copy(k_hi[:, 0, :], rq[:])
                        copy(q_hi[0:HD, 0, :], rk[0:HD, :]).then_inc(stage_hi_done, 1)
                    if s == 8:
                        copy(q_hi[HD:P, 1, :], rk[HD:P, :]).then_inc(stage_hi_done, 1)
                else:
                    if s == 7:
                        scores_used(4)
                        tiles(16)
                        copy(k_hi[:, 0, :], ps[:, PJ, :])
                        copy(q_hi[0:HD, 0, :], ps[0:HD, PJ + 1, :], -HD ** -0.5).then_inc(stage_hi_done, 1)
                    if s == 8:
                        copy(q_hi[HD:P, 1, :], ps[HD:P, PJ + 1, :], -HD ** -0.5).then_inc(stage_hi_done, 1)

            def splits(kind, pair, s):
                for k in SPLITS[kind].get(s, ()):
                    split(kind, pair - PAIR0[kind], k)

            def work(kind, pair, j):
                t = tile_at(kind, j, 1)
                if t is not None:
                    exps(kind, pair, t)
                t = tile_at(kind, j, 3)
                if t is not None:
                    turned(kind, pair, t)
                if j in OUT[kind]:
                    out_low(kind, pair, OUT[kind][j])
                if j == OUT_SPLIT[kind]:
                    out_high(kind, pair)
                if j in VALUES[kind]:
                    values_high(kind, pair, VALUES[kind][j])
                if kind == "c" and j == 5:
                    shift_values(pair)

            def heads(before, kind, pair, after, ahead=None):
                for s in range(SLOTS):
                    if after and s == 0:
                        splits(after, pair + 1, s)
                    if before:
                        work(before, pair - 1, s + SLOTS)
                    work(kind, pair, s)
                    if s == 0:
                        project(kind, pair, SLOTS)
                    if after:
                        project(after, pair + 1, s)
                        if s > 0:
                            splits(after, pair + 1, s)
                    if ahead and s >= 4:
                        split(ahead, 0, s - 4)

            def pairs(kind, n, before, after, ahead=None):
                p0 = PAIR0[kind]
                if before is None:
                    for s in range(SLOTS):
                        splits(kind, p0, s)
                        project(kind, p0, s)
                heads(before, kind, p0, kind)
                with act.Fori(p0 + 1, p0 + n - 1) as pair:
                    heads(kind, kind, pair, kind)
                heads(kind, kind, p0 + n - 1, after, ahead)
                if after is None:
                    for j in range(SLOTS, SPAN):
                        work(kind, p0 + n - 1, j)

            def columns(phase, m0, sq0):
                K = STEP_CHUNKS[phase]
                done = RING if phase in ("eo", "oo") else 0

                def step(i, before):
                    for k in range(K):
                        if before or k >= done:
                            split(phase, i, k)
                        if k == 1 and before:
                            added(i * 2 - 1)
                        if k == K // 2 + 1:
                            added(i * 2)

                def added(m):
                    act.wait_ge(res_done, m + (m0 + 1 + CR_RES))
                    act.wait_ge(acc_done, m + sq0)
                    nc.scalar.activation(sw[:].rearrange("p (k s) -> p k s", k=1), x[:, bass.ds(m, 1), :],
                                         ACT.Square).then_inc(square_done, 1)

                step(0, False)
                with act.Fori(1, 4) as i:
                    step(i, True)
                added(7)

            def ffn(layer):
                phase = f"u{layer}"

                def silu(f):
                    act.wait_ge(tile_used, f * 16 + (TILE0[phase] + 8))
                    act.wait_ge(hid_done, f + (layer * FT + CR_HID))
                    nc.scalar.activation(rq[:], ps[:, 0, :], ACT.Silu).then_inc(silu_done, 1)

                def hidden(f):
                    act.wait_ge(hid_done, f + (layer * FT + 1 + CR_HID))
                    copy(h_hi[:, bass.ds(f, 1), :], rk[:].rearrange("p (k s) -> p k s", k=1)).then_inc(hid_hi_done, 1)

                def step(f, before):
                    split(phase, f, 0)
                    split(phase, f, 1)
                    if before:
                        hidden(f - 1)
                    split(phase, f, 2)
                    split(phase, f, 3)
                    silu(f)

                step(0, False)
                with act.Fori(1, FT) as f:
                    step(f, True)
                hidden(FT - 1)
                columns(f"d{layer}", 8 + 16 * layer, END["f0" if layer == 0 else "f1"])

            act.sem_inc(exp_done, CR_EXP)
            act.sem_inc(silu_done, CR_SILU)
            for k in range(KT):
                act.wait_ge(x_landed, 32)
                square(x[:, k, :], k)
            split("a0", 0, 0)
            split("a0", 0, 1)
            split("a0", 0, 2)
            norm(0)
            for k in range(3, 8):
                split("a0", 0, k)
                if k in (5, 6, 7):
                    m = k - 5
                    act.wait_ge(tile_used, 8 * (m + 1))
                    square(ps[:, PJ + m, :], 8 + m)
                    copy((rq, rk, vT)[m][:], ps[:, PJ + m, :]).then_inc(c_done, 1)
            act.wait_ge(kpe_done, 3)
            for h in range(2):
                last = copy(k_hi[NOPE:QA, h, :], of[NOPE:QA, :])
            last.then_inc(stage_hi_done, 1)
            norm(1)
            norm(2)
            pairs("a", A_PAIRS, None, "b")
            pairs("b", B_PAIRS, "a", None, "eo")
            columns("eo", 0, END["kv"])
            norm(3)
            ffn(0)
            norm(4)
            pairs("c", C_PAIRS, None, None, "oo")
            columns("oo", 16, END["od"])
            norm(5)
            ffn(1)
            norm(6)

        @block.vector
        def _(dve):
            tt, sub, mul, add = nc.vector.tensor_tensor, ALU.subtract, ALU.mult, ALU.add

            def low(out, full, high):
                return tt(out, full, high.bitcast(F32), sub)

            def split(phase, step, k):
                w = PER[phase] * P
                dve.wait_ge(w_hi_ready, step * STEP_CHUNKS[phase] + (CHUNK0[phase] + k + 1))
                low(w_lo[:, k % RING, 0:w], w_raw[:, k % RING, 0:w], w_hi[:, k % RING, 0:w]).then_inc(w_lo_ready, 1)

            def norm(n):
                name = NORMS[n]
                dve.wait_ge(ss_done, n + 1)
                nc.vector.tensor_scalar(mean, ps[:, SC, 0:4], 1.0 / (WIDTH[name] * P), EPS, mul, add).then_inc(mean_done, 1)
                dve.wait_ge(root_done, n + 1)
                nc.vector.reciprocal(rinv, root).then_inc(rinv_done, 1)
                dve.wait_ge(rinv_done, n + 1)
                tt(of[:].rearrange("p (t s) -> p t s", t=4), ident.unsqueeze(1).to_broadcast([P, 4, P]),
                   rinv.unsqueeze(2).to_broadcast([P, 4, P]), mul).then_inc(diag_done, 1)
                dve.wait_ge(rbc_done, n + 1)
                g0 = END[name] - WIDTH[name]
                for k, src in enumerate(norm_src(name)):
                    gk = gain[:, GAIN[name] + k:GAIN[name] + k + 1]
                    if name == "fin":
                        nc.vector.scalar_tensor_tensor(out=src, in0=src, scalar=gk, in1=ps[:, SC + 1, :], op0=mul,
                                                       op1=mul).then_inc(fin_done, 1)
                        continue
                    if g0 + k >= 4:
                        dve.wait_ge(xn_done, g0 + k - 3)
                    nc.vector.scalar_tensor_tensor(out=p[:, (g0 + k) % 4, :], in0=src, scalar=gk, in1=ps[:, SC + 1, :],
                                                   op0=mul, op1=mul).then_inc(xf_done, 1)

            def minima(kind, pair, t):
                dve.wait_ge(score_done, tau(kind, pair) + (t + 1))
                o = ps[:, SC + t % 2, :]
                if kind == "a":
                    nc.vector.tensor_reduce(mn[:, t:t + 1], o, AX, ALU.min).then_inc(min_done, 1)
                    return
                dve.wait_ge(pt_done, tau(kind, pair) + (t + 1))
                n = 2 if kind == "c" else 1
                w = S // n
                if kind == "c" and t % 2 == 0:
                    dve.wait_ge(bias_ready, (pair - 8) * 2 + (t // 2 + 1))
                dve.sem_inc(minima_go, 1)
                for u in range(n):
                    table = tM[:, t % 4, :] if kind == "b" else bt[:, t // 2, BAND_KIND[2 * (t % 2) + u], :]
                    c = n * t + u
                    last = nc.vector.tensor_tensor_reduce(
                        out=p[:, t % 4, u * w:(u + 1) * w], in0=o[:, u * w:(u + 1) * w], in1=table, scale=1.0,
                        scalar=3.0e38, op0=add, op1=ALU.min, accum_out=mn[:, c:c + 1])
                last.then_inc(min_done, 1)

            def inverse(kind, pair, t):
                dve.wait_ge(exp_done, tau(kind, pair) + (t + 1 + CR_EXP))
                n = 2 if kind == "c" else 1
                nc.vector.reciprocal(rden[:, n * t:n * t + n], den[:, n * t:n * t + n]).then_inc(rden_done, 1)

            def turned(kind, pair, t):
                dve.wait_ge(pt_hi_done, tau(kind, pair) + (t + 1))
                src = ps[:, PTB + t % 2, :]
                if kind == "c":
                    sl = slice(t * S, (t + 1) * S)
                    low(pt_lo[:, sl], src, pt_hi[:, sl]).then_inc(pt_lo_done, 1)
                else:
                    qs = slice((t % 4) * P, (t % 4 + 1) * P)
                    low(pt_lo.rearrange("p (k s) -> p k s", k=4)[:, :, qs], src.rearrange("p (k s) -> p k s", k=4),
                        pt_hi.rearrange("p (k s) -> p k s", k=4)[:, :, qs]).then_inc(pt_lo_done, 1)

            def out_sum(pair, h):
                dve.wait_ge(o1_done, pair * 2 + (h + 1))
                if h == 0:
                    dve.wait_ge(o_lo_done, pair + CR_OLO)
                r = slice(h * HD, (h + 1) * HD)
                tt(of[r, :], ps[0:HD, OB, :], to[r, :], add).then_inc(o2_done, 1)

            def values_low(pair, h):
                dve.wait_ge(v_hi_done, pair * 2 + (h + 1))
                src = ps[:, PJ + 2, :].rearrange("p (t h d) -> p t h d", t=4, h=2)
                low(v_st[:, :, h, 1, :], src[:, :, h, :], v_st[:, :, h, 0, :]).then_inc(v_lo_done, 1)

            def project(kind, pair, s):
                step = pair - PAIR0[kind]

                def tiles(n):
                    dve.wait_ge(tile_used, step * STEP_TILES[kind] + (TILE0[kind] + n))

                def stage_hi(h):
                    dve.wait_ge(stage_hi_done, pair * 2 + (h + 2))

                if kind == "a":
                    if s in (2, 3):
                        h, dst = s - 2, (rq, rk)[s - 2]
                        tiles(2 * (h + 1))
                        tt(dst[0:QA, :], ps[0:QA, PJ + h, :], tA[0:QA, 0, :], mul)
                        if h == 1:
                            dve.wait_ge(rope_done, pair * 2 + 1)
                        tt(sw[NOPE:QA, :], ps[QA:P, PJ + h, :], tA[NOPE:QA, 1, :], mul).then_inc(rope_t_done, 1)
                        dve.wait_ge(rope_t_done, pair * 2 + (h + 1))
                        tt(dst[NOPE:QA, :], dst[NOPE:QA, :], sw[NOPE:QA, :], add).then_inc(rope_done, 1)
                    if s in (6, 8):
                        h = 0 if s == 6 else 1
                        stage_hi(h)
                        low(q_lo[0:QA, h, :], (rq, rk)[h][0:QA, :], q_hi[0:QA, h, :])
                        low(k_lo[0:NOPE, h, :], ps[h * NOPE:(h + 1) * NOPE, PJ + 1, :], k_hi[0:NOPE, h, :]
                            ).then_inc(staged, 1)
                    return
                if kind == "b" and s in (3, 5):
                    m = 0 if s == 3 else 1
                    tiles(8 * (m + 1))
                    tt((rq, rk)[m][:], ps[:, PJ + m, :], tB[:, 2 * m, :], mul).then_inc(rope_t_done, 1)
                if s in (7, 8):
                    h = s - 7
                    r = slice(h * HD, (h + 1) * HD)
                    stage_hi(h)
                    if h == 0:
                        low(k_lo[:, 0, :], rq[:] if kind == "b" else ps[:, PJ, :], k_hi[:, 0, :])
                    if kind == "b":
                        low(q_lo[r, h, :], rk[r, :], q_hi[r, h, :]).then_inc(staged, 1)
                    else:
                        nc.vector.scalar_tensor_tensor(out=q_lo[r, h, :], in0=ps[r, PJ + 1, :], scalar=-HD ** -0.5,
                                                       in1=q_hi[r, h, :].bitcast(F32), op0=mul, op1=sub
                                                       ).then_inc(staged, 1)

            def splits(kind, pair, s):
                for k in SPLITS[kind].get(s, ()):
                    split(kind, pair - PAIR0[kind], k)

            def work(kind, pair, j):
                t = tile_at(kind, j, 4)
                if t is not None:
                    turned(kind, pair, t)
                t = tile_at(kind, j, 0)
                if t is not None:
                    minima(kind, pair, t)
                t = tile_at(kind, j, 1)
                if t is not None:
                    inverse(kind, pair, t)
                if j in VALUES[kind]:
                    values_low(pair, VALUES[kind][j])
                if j in OUT[kind]:
                    out_sum(pair, OUT[kind][j])

            def heads(before, kind, pair, after, ahead=None):
                for s in range(SLOTS):
                    if after and s == 0:
                        splits(after, pair + 1, s)
                    if before:
                        work(before, pair - 1, s + SLOTS)
                    work(kind, pair, s)
                    if s == 0:
                        project(kind, pair, SLOTS)
                    if after:
                        if after != kind and s == 7:
                            dve.wait_ge(score_done, 8 * A_PAIRS)
                            pads()
                        project(after, pair + 1, s)
                        if s > 0:
                            splits(after, pair + 1, s)
                    if ahead and s >= 4:
                        split(ahead, 0, s - 4)

            def pairs(kind, n, before, after, ahead=None):
                p0 = PAIR0[kind]
                if before is None:
                    for s in range(SLOTS):
                        splits(kind, p0, s)
                        project(kind, p0, s)
                heads(before, kind, p0, kind)
                with dve.Fori(p0 + 1, p0 + n - 1) as pair:
                    heads(kind, kind, pair, kind)
                heads(kind, kind, p0 + n - 1, after, ahead)
                if after is None:
                    for j in range(SLOTS, SPAN):
                        work(kind, p0 + n - 1, j)

            def pads():
                for t in (q_hi, q_lo):
                    nc.vector.memset(t[HD:P, 0, :].bitcast(F32), 0.0)
                    last = nc.vector.memset(t[0:HD, 1, :].bitcast(F32), 0.0)
                last.then_inc(pads_done, 1)

            def columns(phase, nk):
                K = STEP_CHUNKS[phase]
                done = RING if phase in ("eo", "oo") else 0

                def added(m, u):
                    dve.wait_ge(tile_used, m * nk + (TILE0[phase] + nk))
                    xm = x[:, bass.ds(m, 1), :]
                    tt(xm, ps[:, PTB + u, :].rearrange("p (k s) -> p k s", k=1), xm, add).then_inc(res_done, 1)

                def step(i, before):
                    for k in range(K):
                        if before or k >= done:
                            split(phase, i, k)
                        if k == 1 and before:
                            added(i * 2 - 1, 1)
                        if k == K // 2 + 1:
                            added(i * 2, 0)

                step(0, False)
                with dve.Fori(1, 4) as i:
                    step(i, True)
                added(7, 1)

            def ffn(layer):
                phase = f"u{layer}"

                def hidden(f):
                    dve.wait_ge(silu_done, f + (layer * FT + 1 + CR_SILU))
                    dve.wait_ge(tile_used, f * 16 + (TILE0[phase] + 16))
                    if not isinstance(f, int) or f + layer > 0:
                        dve.wait_ge(hid_lo_done, f + layer * FT)
                    tt(rk[:], ps[:, 1, :], rq[:], mul).then_inc(hid_done, 1)

                def step(f, before):
                    split(phase, f, 0)
                    split(phase, f, 1)
                    if before == "first":
                        hidden(0)
                    elif before:
                        hidden(f - 1)
                    split(phase, f, 2)
                    split(phase, f, 3)

                step(0, False)
                step(1, "first")
                with dve.Fori(2, FT) as f:
                    step(f, True)
                hidden(FT - 1)
                columns(f"d{layer}", FT)

            dve.sem_inc(pt_lo_done, CR_PTL)
            dve.sem_inc(hid_done, CR_HID)
            dve.sem_inc(res_done, CR_RES)
            for k in range(3):
                split("a0", 0, k)
            dve.wait_ge(gain_landed, 16)
            dve.wait_ge(cst_landed, 16)
            norm(0)
            for k in range(3, 8):
                split("a0", 0, k)
            dve.wait_ge(tabA_landed, 16)
            dve.wait_ge(tile_used, 32)
            r = slice(NOPE, QA)
            tt(to[r, :], ps[0:ROPE, OB, :], tA[0:ROPE, 1, :], mul).then_inc(kpe_done, 1)
            tt(of[r, :], ps[ROPE:2 * ROPE, OB, :], tA[QA:P, 0, :], mul).then_inc(kpe_done, 1)
            dve.wait_ge(kpe_done, 2)
            tt(of[r, :], to[r, :], of[r, :], add).then_inc(kpe_done, 1)
            dve.wait_ge(stage_hi_done, 1)
            for h in range(2):
                last = low(k_lo[r, h, :], of[r, :], k_hi[r, h, :])
            last.then_inc(o2_done, 1)
            dve.wait_ge(c_done, 3)
            norm(1)
            norm(2)
            dve.wait_ge(tabB_landed, 16)
            dve.wait_ge(lnc_landed, 16)
            pairs("a", A_PAIRS, None, "b")
            pairs("b", B_PAIRS, "a", None, "eo")
            columns("eo", KT)
            norm(3)
            ffn(0)
            norm(4)
            pads()
            pairs("c", C_PAIRS, None, None, "oo")
            columns("oo", KT)
            norm(5)
            ffn(1)
            norm(6)

        @block.gpsimd
        def _(pool):
            tt, sub, mul, add = nc.gpsimd.tensor_tensor, ALU.subtract, ALU.mult, ALU.add

            def square_add(n):
                pool.wait_ge(square_done, n + 1)
                if not isinstance(n, int) or n >= 1:
                    pool.wait_ge(acc_done, n)
                tt(acc[:], acc[:], sw[:], add).then_inc(acc_done, 1)

            def clear(n):
                pool.wait_ge(ss_done, n + 1)
                nc.gpsimd.memset(acc[:], 0.0).then_inc(acc_zero, 1)
                pool.wait_ge(acc_zero, n + 2)

            def norm_low(n):
                name = NORMS[n]
                g0 = END[name] - WIDTH[name]
                for k, (hi, lo) in enumerate(norm_dst(name)):
                    pool.wait_ge(xn_hi_done, g0 + k + 1)
                    tt(lo, p[:, (g0 + k) % 4, :], hi.bitcast(F32), sub).then_inc(xn_done, 1)

            def normalise(kind, pair, t):
                pool.wait_ge(rden_done, tau(kind, pair) + (t + 1))
                n = 2 if kind == "c" else 1
                pu = p[:, t % 4, :].rearrange("p (n w) -> p n w", n=n)
                r = rden[:, n * t:n * t + n].unsqueeze(2).to_broadcast([P, n, S // n])
                tt(pu, pu, r, mul).then_inc(norm_done, 1)

            def biases(pair, h):
                for kind in range(3):
                    last = tt(bt[:, h, kind, :], cm[:, kind, :], wide[:, h, WIDE_OFF[kind]:WIDE_OFF[kind] + BAND], sub)
                last.then_inc(bias_ready, 1)

            def load_biases(pair):
                pool.dma_start(wide, bias[bass.ds((pair - 8) * 2, 2)].rearrange("h p w -> p h w")).then_inc(bias_landed, 16)

            def project(kind, pair, s):
                if kind == "b" and s in (4, 6):
                    m = 0 if s == 4 else 1
                    pool.wait_ge(swap_done, (pair - 4) * 2 + (m + 1))
                    tt(sw[:], sw[:], tB[:, 2 * m + 1, :], mul).then_inc(rope_m_done, 1)
                    pool.wait_ge(rope_m_done, (pair - 4) * 2 + (m + 1))
                    pool.wait_ge(rope_t_done, pair * 2 + (m + 1))
                    dst = (rq, rk)[m][:]
                    tt(dst, dst, sw[:], add).then_inc(rope_done, 1)
                if kind == "c" and s == 0:
                    pool.wait_ge(bias_ready, (pair - 8) * 2)
                    load_biases(pair)
                if kind == "c" and s in (3, 7):
                    h = s // 4
                    pool.wait_ge(bias_landed, (pair - 7) * 16)
                    pool.wait_ge(min_done, tau(kind, pair) + (2 * h - 2))
                    biases(pair, h)

            def work(kind, pair, j):
                t = tile_at(kind, j, GAP[kind])
                if t is not None:
                    normalise(kind, pair, t)
                if j == OUT_SPLIT[kind]:
                    out_low(kind, pair)

            def heads(before, kind, pair, after):
                for s in range(SLOTS):
                    if before:
                        work(before, pair - 1, s + SLOTS)
                    work(kind, pair, s)
                    if after:
                        project(after, pair + 1, s)

            def out_low(kind, pair):
                pool.wait_ge(o_hi_done, pair + 1)
                k = pair - 8 if kind == "c" else pair
                dst, hi = o_lo[:, bass.ds(k, 1), :], o_hi[:, bass.ds(k, 1), :]
                tt(dst, of[:].rearrange("p (k s) -> p k s", k=1), hi.bitcast(F32), sub).then_inc(o_lo_done, 1)

            def pairs(kind, n, before, after):
                p0 = PAIR0[kind]
                if kind == "c":
                    pool.wait_ge(cmask_landed, 16)
                    pool.wait_ge(bias_landed, 16)
                    biases(p0, 0)
                    biases(p0, 1)
                heads(before, kind, p0, kind)
                with pool.Fori(p0 + 1, p0 + n - 1) as pair:
                    heads(kind, kind, pair, kind)
                heads(kind, kind, p0 + n - 1, after)
                if after is None:
                    for j in range(SLOTS, SPAN):
                        work(kind, p0 + n - 1, j)

            def columns(sq0):
                with pool.Fori(0, 8) as m:
                    square_add(m + sq0)

            def ffn(layer):
                with pool.Fori(0, FT) as f:
                    pool.wait_ge(hid_hi_done, f + (layer * FT + 1))
                    tt(h_lo[:, bass.ds(f, 1), :], rk[:].rearrange("p (k s) -> p k s", k=1),
                       h_hi[:, bass.ds(f, 1), :].bitcast(F32), sub).then_inc(hid_lo_done, 1)
                columns(END["f0" if layer == 0 else "f1"])

            pool.sem_inc(o_lo_done, CR_OLO)
            nc.gpsimd.memset(acc[:], 0.0).then_inc(acc_zero, 1)
            pool.wait_ge(acc_zero, 1)
            for k in range(KT):
                square_add(k)
            clear(0)
            norm_low(0)
            square_add(8)
            square_add(9)
            clear(1)
            square_add(10)
            norm_low(1)
            clear(2)
            norm_low(2)
            pool.wait_ge(tabB_landed, 16)
            pairs("a", A_PAIRS, None, "b")
            pairs("b", B_PAIRS, "a", None)
            columns(END["kv"])
            clear(3)
            norm_low(3)
            pool.dma_start(cm, cmask).then_inc(cmask_landed, 16)
            load_biases(8)
            ffn(0)
            clear(4)
            norm_low(4)
            pairs("c", C_PAIRS, None, None)
            columns(END["od"])
            clear(5)
            norm_low(5)
            ffn(1)
            clear(6)


def _rows(w, cols):
    import numpy as np
    a = np.ascontiguousarray(w[:, cols]) if not isinstance(cols, slice) else w[:, cols]
    if a.shape[1] < P:
        a = np.concatenate([a, np.zeros((a.shape[0], P - a.shape[1]), a.dtype)], axis=1)
    return [a[k * P:(k + 1) * P] for k in range(a.shape[0] // P)]


def _chunks(tiles, per):
    import numpy as np
    zero = np.zeros((P, P), np.float32)
    tiles = [zero if t is None else t for t in tiles]
    a = np.stack(tiles).reshape(len(tiles) // per, per, P, P)
    return np.ascontiguousarray(a.transpose(0, 2, 1, 3).reshape(len(tiles) // per, P, per * P))


def _layout(i):
    import numpy as np
    ar = np.arange
    nat = (ar(S) % 8) * 64 + ar(S) // 8
    w_in, q_up, kv_up = i["ev_w_in"][0], i["ev_w_q_up"][0], i["ev_w_kv_up"][0]
    swap = np.r_[16:32, 0:16]
    t = {}
    kpe = QR + KVR + ar(ROPE)
    t["a0"] = sum([_rows(w_in, ar(m * P, m * P + P)) for m in range(3)], []) + _rows(w_in, np.r_[kpe, kpe[swap]])
    t["a"], t["b"] = [], []
    for pr in range(A_PAIRS):
        for h in (2 * pr, 2 * pr + 1):
            c = h * QA
            t["a"] += _rows(q_up, np.r_[c + ar(QA), c + NOPE + swap])
        c0, c1 = 4 * pr * 64, (4 * pr + 2) * 64
        t["a"] += _rows(kv_up, np.r_[c0 + 64 + ar(64), c1 + 64 + ar(64)]) + [None]
        t["a"] += _rows(kv_up, np.r_[c0 + ar(64), c1 + ar(64)]) + [None]
        for m in (1, 0, 2):
            t["b"] += _rows(w_in, 416 + 512 * m + 128 * pr + ar(P))
    t["eo"] = sum([_rows(i["ev_w_out"][0], m * P + ar(P)) for m in range(8)], [])
    t["oo"] = sum([_rows(i["od_w_out"][0], m * P + ar(P)) for m in range(8)], [])
    t["c"] = sum([_rows(i["od_w_qkv"][0], m * DM + pr * P + ar(P)) for pr in range(8) for m in (1, 0, 2)], [])
    for l in range(2):
        t[f"u{l}"] = sum([_rows(i[w][l], f * P + ar(P)) for f in range(FT) for w in ("ffn_w_gate", "ffn_w_up")], [])
        t[f"d{l}"] = sum([_rows(i["ffn_w_down"][l], m * P + ar(P)) + [None, None] for m in range(8)], [])
    arrays = {f"w_{k}": _chunks(v, PER[k]) for k, v in t.items()}
    arrays["xT"] = np.ascontiguousarray(i["x"][0][nat].T.reshape(KT, P, S).transpose(1, 0, 2))
    g = np.zeros((P, 48), np.float32)
    for name, a in (("ev", i["ev_norm"][0]), ("f0", i["ffn_norm"][0]), ("od", i["od_norm"][0]),
                    ("f1", i["ffn_norm"][1]), ("fin", i["final_norm"]), ("q", i["ev_q_norm"][0]),
                    ("kv", i["ev_kv_norm"][0])):
        a = a.reshape(-1, P).T
        g[:, GAIN[name]:GAIN[name] + a.shape[1]] = a
    arrays["gains"] = g
    arrays["consts"] = np.stack([np.eye(P, dtype=np.float32), np.ones((P, P), np.float32)], axis=1)

    def rope(dim):
        inv = np.float32(10000.0) ** (-np.arange(0, dim, 2, dtype=np.float32) / np.float32(dim))
        ang = nat.astype(np.float32)[None, :] * inv.astype(np.float32)[:, None]
        return np.cos(ang), np.sin(ang)

    ca, sa = rope(ROPE)
    cb, sbn = rope(HD)
    scale = float(QA) ** -0.5
    a = np.zeros((P, 2, S), np.float32)
    a[0:NOPE, 0] = -scale
    a[NOPE:QA, 0] = -scale * np.r_[ca, ca]
    a[QA:, 0] = np.r_[-sa, sa]
    a[0:ROPE, 1] = np.r_[ca, ca]
    a[NOPE:QA, 1] = -scale * np.r_[-sa, sa]
    arrays["tabA"] = a
    C, R = np.tile(np.r_[cb, cb], (2, 1)), np.tile(np.r_[-sbn, sbn], (2, 1))
    arrays["tabB"] = np.ascontiguousarray(np.stack([C, R, -0.125 * C, -0.125 * R], axis=1).astype(np.float32))
    d = np.abs(nat[:, None] - nat[None, :])
    count = sum(((d % dil == 0) & (d // dil <= win // (2 * dil))).astype(np.float32)
                for win, dil in ((128, 1), (512, 4), (2048, 16)))
    lnc = np.where(count > 0, -np.log(np.maximum(count, 1)), 1e30).astype(np.float32)
    arrays["lnc"] = np.ascontiguousarray(lnc.reshape(4, P, S).transpose(1, 0, 2))
    cm = np.zeros((P, 3, BAND), np.float32)
    for kind, j in enumerate((0, 1, 3)):
        qc = 16 * j + np.arange(P) // 8
        kc = BAND_START[j] // 8 + np.arange(BAND) // 8
        start = np.clip(qc - 8, 0, 48)[:, None]
        cm[:, kind] = np.where((kc[None] >= start) & (kc[None] < start + 16), 0.0, 1e30)
    arrays["cmask"] = cm
    rpb = i["od_rpb"][0]
    pad = np.zeros((16, 15, 31 + 17 + 17), np.float32)
    pad[:, :, 17:48] = rpb
    wide = np.zeros((16, P, 48, 8), np.float32)
    for q in range(P):
        qc, r = q // 8, q % 8
        wide[:, q] = pad[:, 7 - r:15 - r, 16 - qc:64 - qc].transpose(0, 2, 1)
    arrays["bias"] = wide.reshape(16, P, WIDE)
    return arrays, nat


def kernel(**inputs):
    import numpy as np
    import concourse.bacc as bacc
    from concourse.bass_utils import run_bass_kernel_spmd

    arrays, nat = _layout({k: np.asarray(v) for k, v in inputs.items()})
    nc = bacc.Bacc("TRN2", target_bir_lowering=False, num_devices=1)
    ap = {k: nc.dram_tensor(f"in_{k}", v.shape, mybir.dt.from_np(v.dtype), kind="ExternalInput").ap()
          for k, v in arrays.items()}
    out = nc.dram_tensor("out_y", (P, KT, S), F32, kind="ExternalOutput").ap()
    build(nc, ap["xT"], ap["gains"], ap["consts"], ap["tabA"], ap["tabB"], ap["lnc"], ap["cmask"], ap["bias"],
          {k: ap[f"w_{k}"] for k in STREAM}, out)
    r = run_bass_kernel_spmd(nc, [{f"in_{k}": v for k, v in arrays.items()}], core_ids=[0])
    y = r.results[0]["out_y"].transpose(1, 0, 2).reshape(DM, S).T
    back = np.empty_like(y)
    back[nat] = y
    return back[None]
```

```python
from contextlib import ExitStack

import concourse.bass as bass
from concourse import mybir

F32 = mybir.dt.float32
F32R = mybir.dt.float32r
ALU = mybir.AluOpType
ACT = mybir.ActivationFunctionType
AX = mybir.AxisListType.X

P = 128
S = 512
DM = 1024
KT = DM // P
HD = 64
NOPE, ROPE = 64, 32
QA = NOPE + ROPE
QR, KVR = 256, 128
DFF = 2816
FT = DFF // P
A_PAIRS = B_PAIRS = 4
C_PAIRS = 8
RING = 4
EPS = 1e-6

STREAM = {
    "a0": (4, 8, 1, 32),
    "a": (2, 16, A_PAIRS, 6),
    "b": (3, 32, B_PAIRS, 24),
    "eo": (4, 16, 4, 16),
    "u0": (4, 4 * FT, FT, 16),
    "d0": (3, 64, 4, 2 * FT),
    "c": (3, 64, C_PAIRS, 24),
    "oo": (4, 16, 4, 16),
    "u1": (4, 4 * FT, FT, 16),
    "d1": (3, 64, 4, 2 * FT),
}
PER = {k: v[0] for k, v in STREAM.items()}
STEP_CHUNKS = {k: v[1] // v[2] for k, v in STREAM.items()}
STEP_TILES = {k: v[3] for k, v in STREAM.items()}
CHUNK0, TILE0 = {}, {}
_c = _t = 0
for _k, (_per, _n, _steps, _tiles) in STREAM.items():
    CHUNK0[_k], TILE0[_k] = _c, _t
    _c, _t = _c + _n, _t + _steps * _tiles


def through(phase, k):
    if phase == "a":
        return [2, 4, 5, 6][k]
    if phase in ("d0", "d1"):
        return (k // 8) * FT + min(3 * (k % 8 + 1), FT)
    return PER[phase] * (k + 1)


USED = [TILE0[ph] + st * STEP_TILES[ph] + through(ph, k)
        for ph, v in STREAM.items() for st in range(v[2]) for k in range(STEP_CHUNKS[ph])]

GAIN = {"ev": 0, "f0": 8, "od": 16, "f1": 24, "fin": 32, "q": 40, "kv": 42}
BAND_START = [0, 64, 192, 256]
BAND_KIND = [0, 1, 1, 2]
WIDE_OFF = [128, 64, 0]
BAND = 256
WIDE = 384


def build(nc, xT, gains, consts, tabA, tabB, lnc, cmask, bias, streams, out):
    ctx = ExitStack()
    with ctx:
        def sb(name, shape, dt=F32):
            return ctx.enter_context(nc.sbuf_tensor(name, shape, dt))

        def sem(name):
            return ctx.enter_context(nc.semaphore(name))

        x = sb("x_res", [P, KT, S])
        xn_hi = sb("xn_hi", [P, KT, S], F32R)
        xn_lo = sb("xn_lo", [P, KT, S], F32R)
        w_raw = sb("w_raw", [P, RING, 4 * P])
        w_hi = sb("w_hi", [P, RING, 4 * P], F32R)
        w_lo = sb("w_lo", [P, RING, 4 * P], F32R)
        shared = sb("shared", [P, 2 * FT * S], F32R)
        gain = sb("gain", [P, 48])
        cst = sb("cst", [P, 2, P])
        tabs = sb("tabs", [P, 10 * S])
        p = sb("p", [P, 4, S])
        rq = sb("rq", [P, S])
        rk = sb("rk", [P, S])
        sw = sb("sw", [P, S])
        vT = sb("vT", [P, S])
        to = sb("to", [P, S])
        of = sb("of", [P, S])
        sq = sb("sq", [P, S])
        small = sb("small", [P, 64])
        ps = ctx.enter_context(nc.psum_tensor("ps", [P, 8, S], F32))

        squares = [sw, sq]
        ident, ones = cst[:, 0, :], cst[:, 1, :]
        PJ, SC, PTB, OB = 0, 3, 5, 7
        mn, den, rden = small[:, 0:16], small[:, 16:32], small[:, 32:48]
        mean, root, rinv = small[:, 48:52], small[:, 52:56], small[:, 56:60]

        def part(off, n):
            return shared[:, off:off + n]

        q_hi = part(0, 2 * S).rearrange("p (h s) -> p h s", h=2)
        q_lo = part(2 * S, 2 * S).rearrange("p (h s) -> p h s", h=2)
        k_hi = part(4 * S, 2 * S).rearrange("p (h s) -> p h s", h=2)
        k_lo = part(6 * S, 2 * S).rearrange("p (h s) -> p h s", h=2)
        v_st = part(8 * S, 2 * S).rearrange("p (t h e d) -> p t h e d", t=4, h=2, e=2)
        pt_hi = part(10 * S, 4 * S)
        pt_lo = part(14 * S, 4 * S)
        cn_hi = part(18 * S, 3 * S).rearrange("p (k s) -> p k s", k=3)
        cn_lo = part(21 * S, 3 * S).rearrange("p (k s) -> p k s", k=3)
        kb_hi = part(18 * S, 4 * S).rearrange("p (k s) -> p k s", k=4)
        kb_lo = part(40 * S, 4 * S).rearrange("p (k s) -> p k s", k=4)
        v_sh = part(18 * S, 3 * S // 2).rearrange("p (t h e d) -> p t h e d", t=3, h=2, e=2)
        o_hi = part(24 * S, 8 * S).rearrange("p (k s) -> p k s", k=8)
        o_lo = part(32 * S, 8 * S).rearrange("p (k s) -> p k s", k=8)
        h_hi = part(0, FT * S).rearrange("p (k s) -> p k s", k=FT)
        h_lo = part(FT * S, FT * S).rearrange("p (k s) -> p k s", k=FT)

        tA = tabs[:, 0:2 * S].rearrange("p (k s) -> p k s", k=2)
        tB = tabs[:, 2 * S:6 * S].rearrange("p (k s) -> p k s", k=4)
        tM = tabs[:, 6 * S:10 * S].rearrange("p (k s) -> p k s", k=4)
        wide = tabs[:, 0:2 * WIDE].rearrange("p (h w) -> p h w", h=2)
        cm = tabs[:, 2 * WIDE:2 * WIDE + 3 * BAND].rearrange("p (k w) -> p k w", k=3)
        bt = tabs[:, 1536:1536 + 6 * BAND].rearrange("p (h k w) -> p h k w", h=2, k=3)

        landed = [sem(f"landed{s}") for s in range(RING)]
        x_landed = [sem(f"x_landed{h}") for h in range(4)]
        gain_landed, cst_landed, tabA_landed, tabB_landed, lnc_landed, cmask_landed, bias_landed, \
            vsh_landed, vsh2_landed = [sem(n) for n in (
                "gain_landed cst_landed tabA_landed tabB_landed lnc_landed cmask_landed bias_landed "
                "vsh_landed vsh2_landed").split()]
        tile_used, ss_done, rbc_done, score_done, pt_done, vt_done, pv_done = [sem(n) for n in (
            "tile_used ss_done rbc_done score_done pt_done vt_done pv_done").split()]
        w_hi_ready, square_done, root_done, xn_hi_done, exp_done, pt_hi_done, vT_done, v_hi_done, o1_done, \
            o_hi_done, c_done, swap_done, kb_hi_done, stage_hi_done, rms_ready, silu_done, hid_hi_done = [sem(n) for n in (
                "w_hi_ready square_done root_done xn_hi_done exp_done pt_hi_done vT_done v_hi_done o1_done "
                "o_hi_done c_done swap_done kb_hi_done stage_hi_done rms_ready silu_done hid_hi_done").split()]
        w_lo_ready, square2_done, sw_zero, mean_done, diag_done, rinv_done, xf_done, min_done, rden_done, \
            pt_lo_done, v_lo_done, o2_done, rope_t_done, staged, kpe_done, scaled, gate_done, up_done, \
            hid_done, res_done, fin_done, minima_go = [sem(n) for n in (
                "w_lo_ready square2_done sw_zero mean_done diag_done rinv_done xf_done min_done rden_done "
                "pt_lo_done v_lo_done o2_done rope_t_done staged kpe_done scaled gate_done up_done hid_done "
                "res_done fin_done minima_go").split()]
        acc_done, q_lo_done, xn_done, norm_done, rope_m_done, rope_done, o_lo_done, bias_ready, hid_lo_done = [
            sem(n) for n in (
                "acc_done q_lo_done xn_done norm_done rope_m_done rope_done o_lo_done bias_ready hid_lo_done").split()]
        stored = sem("stored")

        CR_EXP, CR_PT, CR_PV, CR_PTL, CR_OLO, CR_HID, CR_RES = 2, 4, 2, 2, 1, 1, 2

        SUMS = {"ev": 4, "q": 6, "kv": 7, "f0": 9, "od": 11, "f1": 13, "fin": 15}
        NEXT_NORM = {"eo": ("f0", 3), "d0": ("od", 4), "oo": ("f1", 5)}
        NORMS = ["ev", "q", "kv", "f0", "od", "f1", "fin"]
        WIDTH = {"ev": 8, "q": 2, "kv": 1, "f0": 8, "od": 8, "f1": 8, "fin": 8}
        END = {}
        n_tiles = 0
        for name in NORMS:
            n_tiles += WIDTH[name]
            END[name] = n_tiles

        PROBS = {"eo": 8 * (A_PAIRS + B_PAIRS) + CR_PTL, "oo": 8 * (A_PAIRS + B_PAIRS) + 4 * C_PAIRS + CR_PTL}
        PROBS["d0"], PROBS["d1"] = PROBS["eo"], PROBS["oo"]

        def norm_src(name):
            if name == "q":
                return [rq[:], rk[:]]
            if name == "kv":
                return [vT[:]]
            return [x[:, k, :] for k in range(KT)]

        def norm_dst(name):
            if name == "q":
                return [(cn_hi[:, k, :], cn_lo[:, k, :]) for k in (0, 1)]
            if name == "kv":
                return [(cn_hi[:, 2, :], cn_lo[:, 2, :])]
            return [(xn_hi[:, k, :], xn_lo[:, k, :]) for k in range(KT)]

        SLOTS, SPAN = 8, 15
        NTILES = {"a": 8, "b": 8, "c": 4}
        GAP = {"a": 1, "b": 1, "c": 2}
        PAIR0 = {"a": 0, "b": A_PAIRS, "c": 8}
        PV = {"a": {6: 0, 8: 1, 10: 2, 12: 3}, "c": {7: 0, 11: 1}}
        OUT = {"a": {9: 0, 13: 1}, "c": {8: 0, 12: 1}}
        OUT_SPLIT = {"a": 14, "c": 13}
        VALUES = {"a": {2: 0, 5: 1}, "c": {2: 0, 4: 1}}
        for config in (PV, OUT, OUT_SPLIT, VALUES):
            config["b"] = config["a"]
        SPLITS = {"a": {0: [0], 1: [1], 3: [2], 4: [3]}, "b": {0: [0, 1], 1: [2, 3], 2: [4], 3: [5], 4: [6], 6: [7]},
                  "c": {0: [0, 1], 1: [2, 3], 2: [4], 3: [5], 4: [6], 5: [7]}}
        FILL = {"b": [0, 4, 4, 4, 4, 0, 4, 4], "c": [3] * 8}

        EARLY = 1

        def tile_at(kind, j, lag):
            t, r = divmod(j - lag, GAP[kind])
            return t if r == 0 and 0 <= t < NTILES[kind] else None

        def tau(kind, pair):
            return pair * 4 + 32 if kind == "c" else pair * 8

        def outputs_ahead(kind, pair):
            return pair * 2 + 16 if kind == "c" else pair * 4

        rms, rms_c = vT, sw
        gated = to
        kpe = p[:, 3, :]
        first_squares = [p[:, 0, :], rq, p[:, 1, :], rk, p[:, 2, :], vT, p[:, 3, :], to]

        block = ctx.enter_context(nc.Block())

        @block.sync
        def _(sp):
            for h in range(4):
                sp.dma_start(x[:, 2 * h:2 * h + 2, :], xT[:, 2 * h:2 * h + 2, :]).then_inc(x_landed[h], 16)
                if h == 0:
                    sp.dma_start(cst[:], consts).then_inc(cst_landed, 16)
            sp.dma_start(gain[:], gains).then_inc(gain_landed, 16)
            for name in STREAM:
                per, n = STREAM[name][0:2]
                base, src = CHUNK0[name], streams[name]
                if name == "a0":
                    for c in range(n):
                        if c >= RING:
                            sp.wait_ge(w_lo_ready, c - RING + 1)
                        sp.dma_start(w_raw[:, c % RING, 0:per * P], src[c]).then_inc(landed[c % RING], 16)
                        if c == 3:
                            sp.dma_start(tA, tabA).then_inc(tabA_landed, 16)
                            sp.dma_start(tB, tabB).then_inc(tabB_landed, 16)
                            sp.dma_start(tM, lnc).then_inc(lnc_landed, 16)
                    continue
                with sp.Fori(0, n // RING) as i:
                    for s in range(RING):
                        sp.wait_ge(w_lo_ready, i * RING + (base + s - RING + 1))
                        sp.dma_start(w_raw[:, s, 0:per * P],
                                     src[bass.ds(i * RING + s, 1)].rearrange("c p w -> p (c w)")
                                     ).then_inc(landed[s], 16)
            for k in range(KT):
                sp.wait_ge(fin_done, k + 1)
                sp.dma_start(out[:, k, :], x[:, k, :]).then_inc(stored, 16)
            sp.wait_ge(stored, 16 * KT)

        @block.tensor
        def _(pe):
            mm = nc.tensor.matmul

            def weight_tile(phase, c0, n, bank, rhs, first, final, cols=P):
                per = PER[phase]
                if n % per == 0:
                    pe.wait_ge(w_lo_ready, c0 + (n // per + 1))
                s, o = (n // per) % RING, (n % per) * P
                a, b = w_hi[:, s, o:o + cols], w_lo[:, s, o:o + cols]
                r_hi, r_lo = rhs
                dst = ps[0:cols, bank, :]
                mm(dst, a, r_hi, start=first, stop=False)
                mm(dst, a, r_lo, start=False, stop=False)
                mm(dst, b, r_hi, start=False, stop=final).then_inc(tile_used, 1)

            def first_use(phase, k, end, tiles):
                def operands(n):
                    s, o = (n // PER[phase] + CHUNK0[phase]) % RING, (n % PER[phase]) * P
                    return w_hi[:, s, o:o + P], w_lo[:, s, o:o + P]

                for n, bank in tiles:
                    if n % PER[phase] == 0:
                        pe.wait_ge(w_lo_ready, CHUNK0[phase] + n // PER[phase] + 1)
                pe.wait_ge(xn_hi_done, end - KT + k + 1)
                for n, bank in tiles:
                    a, b = operands(n)
                    mm(ps[:, bank, :], a, xn_hi[:, k, :], start=(k == 0), stop=False)
                    mm(ps[:, bank, :], b, xn_hi[:, k, :], start=False, stop=False)
                pe.wait_ge(xn_done, end - KT + k + 1)
                for n, bank in tiles:
                    mm(ps[:, bank, :], operands(n)[0], xn_lo[:, k, :], start=False, stop=(k == KT - 1)
                       ).then_inc(tile_used, 1)

            def square_sum(src, first=False, final=False):
                for t in range(4):
                    last = mm(ps[:, SC, t:t + 1], src[:, t * P:(t + 1) * P], ones[:, 0:1], start=(first and t == 0),
                              stop=(final and t == 3))
                last.then_inc(ss_done, 1)

            def norm(n):
                pe.wait_ge(diag_done, n + 1)
                for t in range(4):
                    last = mm(ps[:, SC + 1, t * P:(t + 1) * P], ones, of[:, t * P:(t + 1) * P],
                              start=True, stop=True)
                last.then_inc(rbc_done, 1)

            def xn(k):
                return xn_hi[:, k, :], xn_lo[:, k, :]

            def cn(k):
                return cn_hi[:, k, :], cn_lo[:, k, :]

            def values(pair):
                pe.wait_ge(vT_done, pair + 1)
                if not isinstance(pair, int) or pair > 0:
                    pe.wait_ge(v_lo_done, pair * 2)
                for t in range(4):
                    last = nc.tensor.transpose(ps[:, PJ + 2, t * P:(t + 1) * P], vT[:, t * P:(t + 1) * P], ident)
                last.then_inc(vt_done, 1)

            def scores(kind, pair, t):
                half = NTILES[kind] // 2
                rows, h = QA if kind == "a" else P, t // half
                if t % half == 0:
                    pe.wait_ge(staged, pair * 2 + (t // half + 1))
                    if kind == "a":
                        pe.wait_ge(q_lo_done, pair * 2 + (t // half + 1))
                if kind == "a" or (t < 2 and isinstance(pair, int) and pair == A_PAIRS):
                    pe.wait_ge(exp_done, tau(kind, pair) + (t + CR_EXP - 1))
                if kind != "a":
                    pe.wait_ge(min_done, tau(kind, pair) + (t - 1))
                o = ps[:, SC + t % 2, :]
                if kind == "c":
                    for u in range(2):
                        j = 2 * (t % 2) + u
                        ou = o[:, u * BAND:(u + 1) * BAND]
                        qs, ks = slice(j * P, (j + 1) * P), slice(BAND_START[j], BAND_START[j] + BAND)
                        mm(ou, q_hi[:, h, qs], k_hi[:, 0, ks], start=True, stop=False)
                        mm(ou, q_hi[:, h, qs], k_lo[:, 0, ks], start=False, stop=False)
                        last = mm(ou, q_lo[:, h, qs], k_hi[:, 0, ks], start=False, stop=True)
                else:
                    qs = slice((t % 4) * P, (t % 4 + 1) * P)
                    if kind == "a":
                        ks_hi, ks_lo = k_hi[0:rows, h, :], k_lo[0:rows, h, :]
                    else:
                        ks_hi, ks_lo = (kb[:, bass.ds(pair - A_PAIRS, 1), :].rearrange("p k s -> p (k s)")
                                        for kb in (kb_hi, kb_lo))
                    mm(o, q_hi[0:rows, h, qs], ks_hi, start=True, stop=False)
                    mm(o, q_hi[0:rows, h, qs], ks_lo, start=False, stop=False)
                    last = mm(o, q_lo[0:rows, h, qs], ks_hi, start=False, stop=True)
                last.then_inc(score_done, 1)

            def turn(kind, pair, t):
                pe.wait_ge(norm_done, tau(kind, pair) + (t + 1))
                pe.wait_ge(pt_lo_done, tau(kind, pair) + (t + CR_PTL - 1))
                for kt in range(4):
                    last = nc.tensor.transpose(ps[:, PTB + t % 2, kt * P:(kt + 1) * P],
                                               p[:, t % 4, kt * P:(kt + 1) * P], ident)
                last.then_inc(pt_done, 1)

            def outputs(kind, pair, u):
                h, tiles, first = (u, 2 * u + 2, True) if kind == "c" else (u // 2, 2 * u + 2, u % 2 == 0)
                pe.wait_ge(pt_lo_done, tau(kind, pair) + (tiles + CR_PTL))
                if first:
                    pe.wait_ge(o2_done, pair * 2 + (h + 1))
                    pe.wait_ge(v_lo_done, pair * 2 + (h + 1))
                if kind == "c":
                    if h == 0:
                        pe.wait_ge(vsh_landed, (pair - 7) * 16)
                        pe.wait_ge(vsh2_landed, (pair - 7) * 16)
                    def band(v, q0, block, n, first, final):
                        v, o = v.rearrange("p e d -> p (e d)"), ps[:, OB, q0 * P:(q0 + n) * P]
                        c = slice(h * 2 * S + block * P, h * 2 * S + (block + n) * P)
                        mm(o, v, pt_hi[:, c], start=first, stop=False)
                        return mm(o, v, pt_lo[:, c], start=False, stop=final)

                    for j in (0, 3):
                        for kt in range(2):
                            band(v_st[:, (j // 3) * 2 + kt, h], j, j * 2 + kt, 1, kt == 0, kt == 1)
                    band(v_sh[:, 1, h], 1, 3, 2, True, False)
                    band(v_sh[:, 0, h], 1, 2, 1, False, False)
                    last = band(v_sh[:, 2, h], 2, 5, 1, False, True)
                else:
                    q0 = (u % 2) * 2 * P
                    for kt in range(4):
                        v = v_st[:, kt, h].rearrange("p e d -> p (e d)")
                        o, qs = ps[:, OB, q0:q0 + 2 * P], slice(kt * S + q0, kt * S + q0 + 2 * P)
                        mm(o, v, pt_hi[:, qs], start=(kt == 0), stop=False)
                        last = mm(o, v, pt_lo[:, qs], start=False, stop=(kt == 3))
                last.then_inc(pv_done, 1)

            def project(kind, pair, s):
                step = pair - PAIR0[kind]
                c0 = step * STEP_CHUNKS[kind] + CHUNK0[kind]
                later = not isinstance(pair, int) or pair > 0
                if kind == "a":
                    if s == 1:
                        if later:
                            pe.wait_ge(vT_done, pair)
                        else:
                            pe.wait_ge(xn_done, END["q"])
                        for k in range(2):
                            weight_tile("a", c0, k, PJ, cn(k), k == 0, k == 1)
                    elif s == 2:
                        if later:
                            pe.wait_ge(staged, pair * 2)
                        for k in range(2):
                            weight_tile("a", c0, 2 + k, PJ + 1, cn(k), k == 0, k == 1)
                    elif s == 4:
                        if not later:
                            norm(2)
                            pe.wait_ge(xn_done, END["kv"])
                        pe.wait_ge(rope_t_done, pair * 2 + 1)
                        weight_tile("a", c0, 4, PJ, cn(2), True, True)
                    elif s == 5:
                        pe.wait_ge(rope_t_done, pair * 2 + 2)
                        weight_tile("a", c0, 6, PJ + 1, cn(2), True, True)
                    return
                m0 = sum(FILL[kind][:s])
                for m in range(m0, m0 + FILL[kind][s]):
                    if isinstance(pair, int) and pair == 8:
                        if m == 4:
                            residual_sum(1)
                        if m == 10:
                            norm(4)
                        if m < KT:
                            first_use(kind, m, END["od"], [(m, PJ)])
                            continue
                    if m == 0 and isinstance(pair, int) and pair == A_PAIRS:
                        pe.wait_ge(vT_done, pair)
                    if m == 8:
                        pe.wait_ge(staged, pair * 2)
                    if m == 16:
                        pe.wait_ge(v_lo_done, pair * 2)
                    weight_tile(kind, c0, m, PJ + m // KT, xn(m % KT), m % KT == 0, m % KT == KT - 1)

            def work(kind, pair, j):
                t = tile_at(kind, j, 0)
                if t is not None:
                    scores(kind, pair, t)
                t = tile_at(kind, j, 3)
                if t is not None:
                    turn(kind, pair, t)
                if j in PV[kind]:
                    outputs(kind, pair, PV[kind][j])
                if j == 1:
                    values(pair)

            def heads(before, kind, pair, after, early=None):
                for s in range(SLOTS):
                    if before:
                        work(before, pair - 1, s + SLOTS)
                    work(kind, pair, s)
                    if after:
                        project(after, pair + 1, s)
                    elif s >= EARLY:
                        early(s - EARLY)

            def pairs(kind, n, before, after, early=None):
                p0 = PAIR0[kind]
                if before is None:
                    for s in range(SLOTS):
                        project(kind, p0, s)
                heads(before, kind, p0, kind)
                with pe.Fori(p0 + 1, p0 + n - 1) as pair:
                    heads(kind, kind, pair, kind)
                heads(kind, kind, p0 + n - 1, after, early)
                if after is None:
                    for j in range(SLOTS, SPAN):
                        work(kind, p0 + n - 1, j)
                        if j < SPAN - 1:
                            early(j - EARLY)
                        if j == SPAN - 2:
                            early(j + 1 - EARLY)

            def columns(phase, nth, nk, rhs, step0):
                m0 = 8 * nth
                half = PER[phase] * STEP_CHUNKS[phase] // 2

                def tile(i, u):
                    for k in range(nk):
                        weight_tile(phase, i * STEP_CHUNKS[phase] + CHUNK0[phase], u * half + k, PTB + u, rhs(k),
                                    k == 0, k == nk - 1)

                step0()
                pe.wait_ge(pt_lo_done, PROBS[phase])
                tile(1, 0)
                tile(1, 1)
                with pe.Fori(2, 4) as i:
                    for u in range(2):
                        pe.wait_ge(res_done, i * 2 + (m0 + u + 1))
                        tile(i, u)

            def residual_sum(nth):
                pe.wait_ge(acc_done, 6 * nth + 10)
                square_sum(to, True, False)
                pe.wait_ge(square_done, 8 * nth + 15)
                square_sum(squares[1], False, True)

            def heads_out(k):
                return o_hi[:, k, :], o_lo[:, k, :]

            def project_out(phase, pairs_done):
                def early(m):
                    if m == 0:
                        pe.wait_ge(staged, pairs_done * 2)
                        pe.wait_ge(o_lo_done, pairs_done - 2 + CR_OLO)
                    if m == 12:
                        pe.wait_ge(o_lo_done, pairs_done - 1 + CR_OLO)
                    u, k = (m // 6, m % 6) if m < 12 else (m - 12, 6)
                    weight_tile(phase, CHUNK0[phase], m, PJ + u, heads_out(k), k == 0, False)

                def late():
                    pe.wait_ge(o_lo_done, pairs_done + CR_OLO)
                    for u in range(2):
                        weight_tile(phase, CHUNK0[phase], 14 + u, PJ + u, heads_out(7), False, True)
                return early, late

            def hidden_tile(k):
                return h_hi[:, k, :], h_lo[:, k, :]

            def ffn(layer):
                phase = f"u{layer}"
                down = f"d{layer}"
                end = END["f0" if layer == 0 else "f1"]
                for k in range(KT):
                    first_use(phase, k, end, [(2 * k, PJ + 2), (2 * k + 1, OB)])
                    if k == 2:
                        residual_sum(2 * layer)
                    if k == 5:
                        norm(3 + 2 * layer)
                with pe.Fori(1, FT) as f:
                    for g in range(2):
                        pe.wait_ge((gate_done, up_done)[g], f + layer * FT)
                        for k in range(KT):
                            weight_tile(phase, f * 4 + CHUNK0[phase], g * KT + k, g, xn(k), k == 0, k == KT - 1)

                def step0():
                    pe.wait_ge(hid_lo_done, (layer + 1) * FT - 1)
                    for u, bank in enumerate((PJ + 2, OB)):
                        for k in range(FT):
                            if u == 0 and k == FT - 1:
                                pe.wait_ge(hid_lo_done, (layer + 1) * FT)
                            weight_tile(down, CHUNK0[down], u * 24 + k, bank, hidden_tile(k), k == 0, k == FT - 1)

                columns(down, 1 + 2 * layer, FT, hidden_tile, step0)

            pe.sem_inc(pt_done, CR_PT)
            pe.sem_inc(pv_done, CR_PV)
            pe.wait_ge(cst_landed, 16)
            for k in range(0, KT, 2):
                pe.wait_ge(acc_done, k // 2 + 1)
                square_sum(first_squares[k], k == 0, k == KT - 2)
            norm(0)
            for k in range(KT):
                first_use("a0", k, END["ev"], [(2 * k, PJ), (2 * k + 1, PJ + 1)])
            for k in range(KT):
                weight_tile("a0", 0, 16 + k, OB, xn(k), k == 0, k == KT - 1, cols=2 * ROPE)
            for m in range(2):
                pe.wait_ge(square_done, 5 + m)
                square_sum(squares[m], m == 0, m == 1)
            for k in range(KT):
                weight_tile("a0", 0, 24 + k, PJ + 2, xn(k), k == 0, k == KT - 1)
                if k == 3:
                    norm(1)
            pe.wait_ge(square_done, 7)
            square_sum(squares[0], True, True)
            pairs("a", A_PAIRS, None, "b")
            early, late = project_out("eo", 8)
            pairs("b", B_PAIRS, "a", None, early)
            columns("eo", 0, KT, heads_out, late)
            ffn(0)
            early, late = project_out("oo", 16)
            pairs("c", C_PAIRS, None, None, early)
            columns("oo", 2, KT, heads_out, late)
            ffn(1)
            residual_sum(3)
            norm(6)

        @block.scalar
        def _(act):
            def copy(out, in_, scale=1.0):
                return nc.scalar.activation(out, in_, ACT.Copy, scale=scale)

            def split(phase, step, k):
                per, w = PER[phase], PER[phase] * P
                c = step * STEP_CHUNKS[phase] + (CHUNK0[phase] + k)
                act.wait_ge(landed[k % RING], chunk_bytes(phase, step, k))
                if isinstance(step, int):
                    if c >= RING:
                        act.wait_ge(tile_used, USED[c - RING])
                else:
                    K = STEP_CHUNKS[phase]
                    j = k - RING
                    back = through(phase, j) if j >= 0 else through(phase, j + K) - STEP_TILES[phase]
                    act.wait_ge(tile_used, step * STEP_TILES[phase] + (TILE0[phase] + back))
                copy(w_hi[:, k % RING, 0:w], w_raw[:, k % RING, 0:w]).then_inc(w_hi_ready, 1)

            def chunk_bytes(phase, step, k):
                K = STEP_CHUNKS[phase]
                return step * (16 * K // RING) + 16 * ((CHUNK0[phase] + k) // RING + 1)

            def take_root(n):
                act.wait_ge(mean_done, n + 1)
                nc.scalar.activation(root, mean, ACT.Sqrt).then_inc(root_done, 1)

            def keep_rms(n, dst):
                act.wait_ge(rbc_done, n + 1)
                copy(dst[:], ps[:, SC + 1, :]).then_inc(rms_ready, 1)

            def highs(n):
                name = NORMS[n]
                g0 = END[name] - WIDTH[name]
                for k, (hi, lo) in enumerate(norm_dst(name)):
                    act.wait_ge(xf_done, g0 + k + 1)
                    copy(hi, p[:, (g0 + k) % 4, :]).then_inc(xn_hi_done, 1)

            def norm(n, ahead):
                take_root(n)
                split(ahead, 0, 3)
                highs(n)

            def exps(kind, pair, t):
                act.wait_ge(min_done, tau(kind, pair) + (t + 1))
                if kind == "a":
                    act.wait_ge(pt_done, tau(kind, pair) + (t + 1))
                    nc.scalar.activation(p[:, t % 4, :], ps[:, SC + t % 2, :], ACT.Exp, bias=mn[:, t:t + 1], scale=-1.0,
                                         accum_out=den[:, t:t + 1]).then_inc(exp_done, 1)
                    return
                n = 2 if kind == "c" else 1
                w = S // n
                for u in range(n):
                    c = n * t + u
                    pu = p[:, t % 4, u * w:(u + 1) * w]
                    last = nc.scalar.activation(pu, pu, ACT.Exp, bias=mn[:, c:c + 1], scale=-1.0,
                                                accum_out=den[:, c:c + 1])
                last.then_inc(exp_done, 1)

            def turned(kind, pair, t):
                act.wait_ge(pt_done, tau(kind, pair) + (t + 1 + CR_PT))
                if t % 2 == 0:
                    act.wait_ge(pv_done, outputs_ahead(kind, pair) + (t // 2 + 1))
                src = ps[:, PTB + t % 2, :]
                if kind == "c":
                    copy(pt_hi[:, t * S:(t + 1) * S], src).then_inc(pt_hi_done, 1)
                else:
                    dst = pt_hi.rearrange("p (k s) -> p k s", k=4)[:, :, (t % 4) * P:(t % 4 + 1) * P]
                    copy(dst, src.rearrange("p (k s) -> p k s", k=4)).then_inc(pt_hi_done, 1)

            def out_low(kind, pair, h):
                n = h + 1 if kind == "c" else 2 * h + 2
                act.wait_ge(pv_done, outputs_ahead(kind, pair) + (n + CR_PV))
                copy(to[h * HD:(h + 1) * HD, :], ps[HD:P, OB, :]).then_inc(o1_done, 1)

            def out_high(kind, pair):
                act.wait_ge(o2_done, pair * 2 + 3)
                k = pair - 8 if kind == "c" else pair
                copy(o_hi[:, bass.ds(k, 1), :], of[:].rearrange("p (k s) -> p k s", k=1)).then_inc(o_hi_done, 1)

            def values_high(kind, pair, h):
                if h == 0:
                    act.wait_ge(vt_done, pair + 1)
                else:
                    act.wait_ge(v_lo_done, pair * 2 + 1)
                if kind == "c":
                    act.wait_ge(pv_done, outputs_ahead(kind, pair) + (h + 1))
                elif not isinstance(pair, int) or pair > 0:
                    act.wait_ge(pv_done, outputs_ahead(kind, pair) + 2 * h)
                src = ps[:, PJ + 2, :].rearrange("p (t h d) -> p t h d", t=4, h=2)
                copy(v_st[:, :, h, 0, :], src[:, :, h, :]).then_inc(v_hi_done, 1)

            def shift_values(pair):
                act.wait_ge(v_lo_done, pair * 2 + 2)
                flat = v_st.rearrange("p t h e d -> p t (h e d)")
                dst = v_sh.rearrange("p t h e d -> p t (h e d)")
                act.dma_start(dst[0:HD].bitcast(F32), flat[HD:P, 0:3].bitcast(F32)).then_inc(vsh_landed, 16)
                act.dma_start(dst[HD:P].bitcast(F32), flat[0:HD, 1:4].bitcast(F32)).then_inc(vsh2_landed, 16)

            def project(kind, pair, s):
                step = pair - PAIR0[kind]

                def tiles(n):
                    act.wait_ge(tile_used, step * STEP_TILES[kind] + (TILE0[kind] + n))

                def scores_used(n):
                    if not (isinstance(pair, int) and pair in (0, 8)):
                        act.wait_ge(score_done, tau(kind, pair) + (n - NTILES[kind]))

                if kind == "a":
                    if s == 5:
                        tiles(5)
                        copy(vT[:], ps[:, PJ, :]).then_inc(vT_done, 1)
                    if s in (6, 8):
                        h = 0 if s == 6 else 1
                        scores_used(4 * (h + 1))
                        act.wait_ge(rope_done, pair * 2 + (h + 1))
                        copy(q_hi[:, h, :], (rq, rk)[h][:])
                        tiles(6)
                        copy(k_hi[0:NOPE, h, :], ps[h * NOPE:(h + 1) * NOPE, PJ + 1, :]).then_inc(stage_hi_done, 1)
                    return
                if kind == "b":
                    if s == 8:
                        tiles(24)
                        copy(vT[:], ps[:, PJ + 2, :]).then_inc(vT_done, 1)
                    if s in (3, 5):
                        m = 0 if s == 3 else 1
                        tiles(8 * (m + 1))
                        act.wait_ge(rope_done, pair * 2 + m)
                        act.wait_ge(rope_t_done, pair * 2 + (m + 1))
                        for g in range(4):
                            last = copy(sw[32 * g:32 * g + 32, :], ps[32 * (g ^ 1):32 * (g ^ 1) + 32, PJ + m, :])
                        last.then_inc(swap_done, 1)
                    if s == 6:
                        act.wait_ge(rope_done, pair * 2 + 1)
                        copy(kb_hi[:, bass.ds(step, 1), :], rq[:].rearrange("p (k s) -> p k s", k=1)
                             ).then_inc(kb_hi_done, 1)
                    if s == 7:
                        scores_used(4)
                        act.wait_ge(rope_done, pair * 2 + 2)
                        copy(q_hi[0:HD, 0, :], rk[0:HD, :]).then_inc(stage_hi_done, 1)
                    if s == 8:
                        copy(q_hi[HD:P, 1, :], rk[HD:P, :]).then_inc(stage_hi_done, 1)
                else:
                    if s == 7:
                        scores_used(4)
                        act.wait_ge(scaled, step * 2 + 2)
                        copy(k_hi[:, 0, :], rq[:])
                        copy(q_hi[0:HD, 0, :], rk[0:HD, :], -HD ** -0.5).then_inc(stage_hi_done, 1)
                    if s == 8:
                        copy(q_hi[HD:P, 1, :], rk[HD:P, :], -HD ** -0.5).then_inc(stage_hi_done, 1)

            def splits(kind, pair, s, done=0):
                for k in SPLITS[kind].get(s, ()):
                    if k >= done:
                        split(kind, pair - PAIR0[kind], k)

            def work(kind, pair, j):
                t = tile_at(kind, j, 1)
                if t is not None:
                    exps(kind, pair, t)
                t = tile_at(kind, j, 3)
                if t is not None:
                    turned(kind, pair, t)
                if j in OUT[kind]:
                    out_low(kind, pair, OUT[kind][j])
                if j == OUT_SPLIT[kind]:
                    out_high(kind, pair)
                if j in VALUES[kind]:
                    values_high(kind, pair, VALUES[kind][j])
                if kind == "c" and j == 5:
                    shift_values(pair)

            def heads(before, kind, pair, after, ahead=None):
                for s in range(SLOTS):
                    if after and s == 0:
                        splits(after, pair + 1, s)
                    if before:
                        work(before, pair - 1, s + SLOTS)
                    work(kind, pair, s)
                    if s == 0:
                        project(kind, pair, SLOTS)
                    if after:
                        if s > 0:
                            splits(after, pair + 1, s)
                        project(after, pair + 1, s)
                    if ahead and s < RING:
                        split(ahead, 0, s)

            def pairs(kind, n, before, after, ahead=None):
                p0 = PAIR0[kind]
                if before is None:
                    for s in range(SLOTS):
                        splits(kind, p0, s, RING)
                        if kind == "c" and s == 3:
                            keep_rms(4, rms_c)
                        project(kind, p0, s)
                heads(before, kind, p0, kind)
                with act.Fori(p0 + 1, p0 + n - 1) as pair:
                    heads(kind, kind, pair, kind)
                heads(kind, kind, p0 + n - 1, after, ahead)
                if after is None:
                    for j in range(SLOTS, SPAN):
                        work(kind, p0 + n - 1, j)

            def columns(phase, nth, ahead):
                K = STEP_CHUNKS[phase]
                done = RING if phase in ("eo", "oo") else 2

                def square(m, u):
                    act.wait_ge(res_done, m + (8 * nth + 1 + CR_RES))
                    if not isinstance(m, int) or m >= 2:
                        back = 1 if isinstance(m, int) and m == 2 else 2
                        act.wait_ge(acc_done, m + (6 * nth + 4 - back))
                    nc.scalar.activation(squares[u][:].rearrange("p (k s) -> p k s", k=1), x[:, bass.ds(m, 1), :],
                                         ACT.Square).then_inc(square_done, 1)

                def step(i):
                    for k in range(K):
                        split(phase, i, k)
                        if k == 1:
                            if isinstance(i, int):
                                square(0, 0)
                            square(i * 2 - 1, 1)
                        if k == K // 2 + 1:
                            square(i * 2, 0)

                def high(m):
                    g = GAIN[NEXT_NORM[phase][0]] + m
                    nc.scalar.activation(xn_hi[:, m, :], x[:, m, :], ACT.Copy, scale=gain[:, g:g + 1]
                                         ).then_inc(xn_hi_done, 1)

                for k in range(done, K):
                    split(phase, 0, k)
                step(1)
                if ahead:
                    for m in range(3):
                        high(m)
                with act.Fori(2, 4) as i:
                    step(i)
                nc.scalar.preload_act_table(ACT.Sqrt)
                if ahead:
                    for k in range(3):
                        split(ahead, 0, k)
                        high(3 + k)
                    high(6)
                square(7, 1)
                if ahead:
                    high(7)
                    split(ahead, 0, 3)
                    take_root(3 + nth)

            def ffn(layer):
                phase = f"u{layer}"

                def silu(f):
                    act.wait_ge(gate_done, f + (layer * FT + 1))
                    act.wait_ge(hid_done, f + (layer * FT + CR_HID))
                    nc.scalar.activation(rq[:], gated[:], ACT.Silu).then_inc(silu_done, 1)

                def hidden(f):
                    act.wait_ge(hid_done, f + (layer * FT + 1 + CR_HID))
                    copy(h_hi[:, bass.ds(f, 1), :], rk[:].rearrange("p (k s) -> p k s", k=1)).then_inc(hid_hi_done, 1)

                def step(f):
                    if not isinstance(f, int):
                        split(phase, f, 0)
                        split(phase, f, 1)
                    hidden(f - 1)
                    split(phase, f, 2)
                    split(phase, f, 3)
                    silu(f)

                keep_rms(3 + 2 * layer, rms)
                split(phase, 1, 0)
                split(phase, 1, 1)
                silu(0)
                step(1)
                with act.Fori(2, FT) as f:
                    step(f)
                split(f"d{layer}", 0, 0)
                split(f"d{layer}", 0, 1)
                hidden(FT - 1)
                columns(f"d{layer}", 1 + 2 * layer, "c" if layer == 0 else None)

            act.sem_inc(exp_done, CR_EXP)
            for k in range(0, KT, 2):
                act.wait_ge(x_landed[k // 2], 16)
                nc.scalar.activation(first_squares[k], x[:, k, :], ACT.Square).then_inc(square_done, 1)
            nc.scalar.preload_act_table(ACT.Sqrt)
            for k in range(3):
                split("a0", 0, k)
            norm(0, "a0")
            for k in range(4, 7):
                split("a0", 0, k)
            act.wait_ge(tile_used, 16)
            for m in range(2):
                nc.scalar.activation(squares[m][:], ps[:, PJ + m, :], ACT.Square).then_inc(square_done, 1)
                copy((rq, rk)[m][:], ps[:, PJ + m, :]).then_inc(c_done, 1)
            split("a0", 0, 7)
            take_root(1)
            split("a", 0, 0)
            split("a", 0, 1)
            highs(1)
            act.wait_ge(tile_used, 32)
            act.wait_ge(ss_done, SUMS["q"])
            nc.scalar.activation(sw[:], ps[:, PJ + 2, :], ACT.Square).then_inc(square_done, 1)
            copy(vT[:], ps[:, PJ + 2, :]).then_inc(c_done, 1)
            take_root(2)
            act.wait_ge(kpe_done, 3)
            for h in range(2):
                last = copy(k_hi[NOPE:QA, h, :], kpe[NOPE:QA, :])
            last.then_inc(stage_hi_done, 1)
            split("a", 0, 2)
            split("a", 0, 3)
            highs(2)
            pairs("a", A_PAIRS, None, "b")
            pairs("b", B_PAIRS, "a", None, "eo")
            columns("eo", 0, "u0")
            ffn(0)
            pairs("c", C_PAIRS, None, None, "oo")
            columns("oo", 2, "u1")
            ffn(1)
            take_root(6)

        @block.vector
        def _(dve):
            tt, sub, mul, add = nc.vector.tensor_tensor, ALU.subtract, ALU.mult, ALU.add

            def low(out, full, high):
                return tt(out, full, high.bitcast(F32), sub)

            def split(phase, step, k):
                w = PER[phase] * P
                dve.wait_ge(w_hi_ready, step * STEP_CHUNKS[phase] + (CHUNK0[phase] + k + 1))
                low(w_lo[:, k % RING, 0:w], w_raw[:, k % RING, 0:w], w_hi[:, k % RING, 0:w]).then_inc(w_lo_ready, 1)

            def inverse_rms(n):
                name = NORMS[n]
                dve.wait_ge(ss_done, SUMS[name])
                nc.vector.tensor_scalar(mean, ps[:, SC, 0:4], 1.0 / (WIDTH[name] * P), EPS, mul, add).then_inc(mean_done, 1)
                dve.wait_ge(root_done, n + 1)
                nc.vector.reciprocal(rinv, root).then_inc(rinv_done, 1)
                dve.wait_ge(rinv_done, n + 1)
                tt(of[:].rearrange("p (t s) -> p t s", t=4), ident.unsqueeze(1).to_broadcast([P, 4, P]),
                   rinv.unsqueeze(2).to_broadcast([P, 4, P]), mul).then_inc(diag_done, 1)

            def normed(n):
                name = NORMS[n]
                dve.wait_ge(rbc_done, n + 1)
                g0 = END[name] - WIDTH[name]
                for k, src in enumerate(norm_src(name)):
                    gk = gain[:, GAIN[name] + k:GAIN[name] + k + 1]
                    if name == "fin":
                        nc.vector.scalar_tensor_tensor(out=src, in0=src, scalar=gk, in1=ps[:, SC + 1, :], op0=mul,
                                                       op1=mul).then_inc(fin_done, 1)
                        continue
                    if g0 + k >= 4:
                        dve.wait_ge(xn_done, g0 + k - 3)
                    nc.vector.scalar_tensor_tensor(out=p[:, (g0 + k) % 4, :], in0=src, scalar=gk, in1=ps[:, SC + 1, :],
                                                   op0=mul, op1=mul).then_inc(xf_done, 1)

            def norm(n, ahead):
                inverse_rms(n)
                if ahead:
                    split(ahead, 0, 3)
                normed(n)

            def minima(kind, pair, t):
                dve.wait_ge(score_done, tau(kind, pair) + (t + 1))
                o = ps[:, SC + t % 2, :]
                if kind == "a":
                    nc.vector.tensor_reduce(mn[:, t:t + 1], o, AX, ALU.min).then_inc(min_done, 1)
                    return
                dve.wait_ge(pt_done, tau(kind, pair) + (t + 1))
                n = 2 if kind == "c" else 1
                w = S // n
                if kind == "c" and t % 2 == 0:
                    dve.wait_ge(bias_ready, (pair - 8) * 2 + (t // 2 + 1))
                dve.sem_inc(minima_go, 1)
                for u in range(n):
                    table = tM[:, t % 4, :] if kind == "b" else bt[:, t // 2, BAND_KIND[2 * (t % 2) + u], :]
                    c = n * t + u
                    last = nc.vector.tensor_tensor_reduce(
                        out=p[:, t % 4, u * w:(u + 1) * w], in0=o[:, u * w:(u + 1) * w], in1=table, scale=1.0,
                        scalar=3.0e38, op0=add, op1=ALU.min, accum_out=mn[:, c:c + 1])
                last.then_inc(min_done, 1)

            def inverse(kind, pair, t):
                dve.wait_ge(exp_done, tau(kind, pair) + (t + 1 + CR_EXP))
                n = 2 if kind == "c" else 1
                nc.vector.reciprocal(rden[:, n * t:n * t + n], den[:, n * t:n * t + n]).then_inc(rden_done, 1)

            def turned(kind, pair, t):
                dve.wait_ge(pt_hi_done, tau(kind, pair) + (t + 1))
                src = ps[:, PTB + t % 2, :]
                if kind == "c":
                    sl = slice(t * S, (t + 1) * S)
                    low(pt_lo[:, sl], src, pt_hi[:, sl]).then_inc(pt_lo_done, 1)
                else:
                    qs = slice((t % 4) * P, (t % 4 + 1) * P)
                    low(pt_lo.rearrange("p (k s) -> p k s", k=4)[:, :, qs], src.rearrange("p (k s) -> p k s", k=4),
                        pt_hi.rearrange("p (k s) -> p k s", k=4)[:, :, qs]).then_inc(pt_lo_done, 1)

            def out_sum(pair, h):
                dve.wait_ge(o1_done, pair * 2 + (h + 1))
                if h == 0:
                    dve.wait_ge(o_lo_done, pair + CR_OLO)
                r = slice(h * HD, (h + 1) * HD)
                tt(of[r, :], ps[0:HD, OB, :], to[r, :], add).then_inc(o2_done, 1)

            def values_low(pair, h):
                dve.wait_ge(v_hi_done, pair * 2 + (h + 1))
                src = ps[:, PJ + 2, :].rearrange("p (t h d) -> p t h d", t=4, h=2)
                low(v_st[:, :, h, 1, :], src[:, :, h, :], v_st[:, :, h, 0, :]).then_inc(v_lo_done, 1)

            def project(kind, pair, s):
                step = pair - PAIR0[kind]

                def tiles(n):
                    dve.wait_ge(tile_used, step * STEP_TILES[kind] + (TILE0[kind] + n))

                def stage_hi(h):
                    dve.wait_ge(stage_hi_done, pair * 2 + (h + 2))

                if kind == "a":
                    if s in (2, 3):
                        h, dst = s - 2, (rq, rk)[s - 2]
                        tiles(2 * (h + 1))
                        if not isinstance(pair, int) or pair > 0:
                            dve.wait_ge(q_lo_done, pair * 2 + (h - 1))
                        tt(dst[0:QA, :], ps[0:QA, PJ + h, :], tA[0:QA, 0, :], mul)
                        if h == 1:
                            dve.wait_ge(rope_done, pair * 2 + 1)
                        tt(sw[NOPE:QA, :], ps[QA:P, PJ + h, :], tA[NOPE:QA, 1, :], mul).then_inc(rope_t_done, 1)
                    if s in (6, 8):
                        h = 0 if s == 6 else 1
                        stage_hi(h)
                        low(k_lo[0:NOPE, h, :], ps[h * NOPE:(h + 1) * NOPE, PJ + 1, :], k_hi[0:NOPE, h, :]
                            ).then_inc(staged, 1)
                    return
                if kind == "b" and s in (3, 5):
                    m = 0 if s == 3 else 1
                    tiles(8 * (m + 1))
                    if isinstance(pair, int) and pair == A_PAIRS:
                        dve.wait_ge(q_lo_done, 2 * A_PAIRS)
                    tt((rq, rk)[m][:], ps[:, PJ + m, :], tB[:, 2 * m, :], mul).then_inc(rope_t_done, 1)
                if kind == "b" and s == 6:
                    dve.wait_ge(kb_hi_done, step + 1)
                    k = bass.ds(step, 1)
                    low(kb_lo[:, k, :], rq[:].rearrange("p (k s) -> p k s", k=1), kb_hi[:, k, :])
                if kind == "c" and s in (3, 6, 8):
                    m, dst = {3: (0, rq), 6: (1, rk), 8: (2, vT)}[s]
                    tiles(8 * (m + 1))
                    if s == 3 and isinstance(pair, int) and pair == 8:
                        dve.wait_ge(rms_ready, 2)
                    tt(dst[:], ps[:, PJ + m, :], rms_c[:], mul).then_inc(vT_done if m == 2 else scaled, 1)
                if s in (7, 8):
                    h = s - 7
                    r = slice(h * HD, (h + 1) * HD)
                    stage_hi(h)
                    if h == 0 and kind == "c":
                        low(k_lo[:, 0, :], rq[:], k_hi[:, 0, :])
                    if kind == "b":
                        low(q_lo[r, h, :], rk[r, :], q_hi[r, h, :]).then_inc(staged, 1)
                    else:
                        nc.vector.scalar_tensor_tensor(out=q_lo[r, h, :], in0=rk[r, :], scalar=-HD ** -0.5,
                                                       in1=q_hi[r, h, :].bitcast(F32), op0=mul, op1=sub
                                                       ).then_inc(staged, 1)

            def splits(kind, pair, s, done=0):
                for k in SPLITS[kind].get(s, ()):
                    if k >= done:
                        split(kind, pair - PAIR0[kind], k)

            def work(kind, pair, j):
                t = tile_at(kind, j, 4)
                if t is not None:
                    turned(kind, pair, t)
                t = tile_at(kind, j, 0)
                if t is not None:
                    minima(kind, pair, t)
                t = tile_at(kind, j, 1)
                if t is not None:
                    inverse(kind, pair, t)
                if j in VALUES[kind]:
                    values_low(pair, VALUES[kind][j])
                if j in OUT[kind]:
                    out_sum(pair, OUT[kind][j])

            def heads(before, kind, pair, after, ahead=None):
                for s in range(SLOTS):
                    if after and s == 0:
                        splits(after, pair + 1, s)
                    if before:
                        work(before, pair - 1, s + SLOTS)
                    work(kind, pair, s)
                    if s == 0:
                        project(kind, pair, SLOTS)
                    if after:
                        if s > 0:
                            splits(after, pair + 1, s)
                        if after != kind and s == 7:
                            dve.wait_ge(score_done, 8 * A_PAIRS)
                            pads()
                        project(after, pair + 1, s)
                    if ahead and s < RING:
                        split(ahead, 0, s)

            def pairs(kind, n, before, after, ahead=None):
                p0 = PAIR0[kind]
                if before is None:
                    for s in range(SLOTS):
                        splits(kind, p0, s, RING)
                        project(kind, p0, s)
                heads(before, kind, p0, kind)
                with dve.Fori(p0 + 1, p0 + n - 1) as pair:
                    heads(kind, kind, pair, kind)
                heads(kind, kind, p0 + n - 1, after, ahead)
                if after is None:
                    for j in range(SLOTS, SPAN):
                        work(kind, p0 + n - 1, j)

            def pads():
                for t in (q_hi, q_lo):
                    nc.vector.memset(t[HD:P, 0, :].bitcast(F32), 0.0)
                    nc.vector.memset(t[0:HD, 1, :].bitcast(F32), 0.0)

            def columns(phase, nk, banks, ahead):
                K = STEP_CHUNKS[phase]
                done = RING if phase in ("eo", "oo") else 2

                def added(m, bank):
                    dve.wait_ge(tile_used, m * nk + (TILE0[phase] + nk))
                    xm = x[:, bass.ds(m, 1), :]
                    tt(xm, ps[:, bank, :].rearrange("p (k s) -> p k s", k=1), xm, add).then_inc(res_done, 1)

                def step(i):
                    for k in range(K):
                        split(phase, i, k)
                        if k == 1:
                            if isinstance(i, int):
                                dve.wait_ge(tile_used, 2 * nk + TILE0[phase])
                                added(0, banks[0])
                                added(1, banks[1])
                            else:
                                added(i * 2 - 1, PTB + 1)
                        if k == K // 2 + 1:
                            added(i * 2, PTB)

                def low_part(m):
                    name = NEXT_NORM[phase][0]
                    dve.wait_ge(xn_hi_done, END[name] - KT + m + 1)
                    nc.vector.scalar_tensor_tensor(out=xn_lo[:, m, :], in0=x[:, m, :],
                                                   scalar=gain[:, GAIN[name] + m:GAIN[name] + m + 1],
                                                   in1=xn_hi[:, m, :].bitcast(F32), op0=mul, op1=sub
                                                   ).then_inc(xn_done, 1)

                for k in range(done, K):
                    split(phase, 0, k)
                step(1)
                if ahead:
                    for m in range(3):
                        low_part(m)
                with dve.Fori(2, 4) as i:
                    step(i)
                if ahead:
                    for k in range(3):
                        split(ahead, 0, k)
                        low_part(3 + k)
                    low_part(6)
                added(7, PTB + 1)
                if ahead:
                    low_part(7)
                    split(ahead, 0, 3)
                    inverse_rms(NEXT_NORM[phase][1])

            def ffn(layer):
                phase = f"u{layer}"

                def gate(f):
                    first = isinstance(f, int) and f == 0
                    dve.wait_ge(tile_used, f * 16 + (TILE0[phase] + (15 if first else 8)))
                    if not first or layer > 0:
                        dve.wait_ge(silu_done, f + layer * FT)
                    tt(gated[:], ps[:, PJ + 2 if first else 0, :], rms[:], mul).then_inc(gate_done, 1)

                def hidden(f):
                    first = isinstance(f, int) and f == 0
                    dve.wait_ge(tile_used, f * 16 + (TILE0[phase] + 16))
                    if not first or layer > 0:
                        dve.wait_ge(hid_lo_done, f + layer * FT)
                    tt(rk[:], ps[:, OB if first else 1, :], rms[:], mul).then_inc(up_done, 1)
                    dve.wait_ge(silu_done, f + (layer * FT + 1))
                    dve.wait_ge(up_done, f + (layer * FT + 1))
                    tt(rk[:], rk[:], rq[:], mul).then_inc(hid_done, 1)

                def step(f, before):
                    if not isinstance(f, int):
                        split(phase, f, 0)
                        split(phase, f, 1)
                    hidden(before)
                    split(phase, f, 2)
                    split(phase, f, 3)
                    gate(f)

                split(phase, 1, 0)
                split(phase, 1, 1)
                dve.wait_ge(rms_ready, 2 * layer + 1)
                gate(0)
                step(1, 0)
                with dve.Fori(2, FT) as f:
                    step(f, f - 1)
                split(f"d{layer}", 0, 0)
                split(f"d{layer}", 0, 1)
                hidden(FT - 1)
                columns(f"d{layer}", FT, (PJ + 2, OB), "c" if layer == 0 else None)

            dve.sem_inc(pt_lo_done, CR_PTL)
            dve.sem_inc(hid_done, CR_HID)
            dve.sem_inc(res_done, CR_RES)
            for k in range(1, KT, 2):
                dve.wait_ge(x_landed[k // 2], 16)
                tt(first_squares[k][:], x[:, k, :], x[:, k, :], mul).then_inc(square2_done, 1)
            for k in range(3):
                split("a0", 0, k)
            dve.wait_ge(gain_landed, 16)
            dve.wait_ge(cst_landed, 16)
            norm(0, "a0")
            for k in range(4, 8):
                split("a0", 0, k)
            inverse_rms(1)
            dve.wait_ge(tabA_landed, 16)
            dve.wait_ge(tile_used, 24)
            r = slice(NOPE, QA)
            tt(to[r, :], ps[0:ROPE, OB, :], tA[0:ROPE, 1, :], mul).then_inc(kpe_done, 1)
            tt(kpe[r, :], ps[ROPE:2 * ROPE, OB, :], tA[QA:P, 0, :], mul).then_inc(kpe_done, 1)
            dve.wait_ge(kpe_done, 2)
            tt(kpe[r, :], to[r, :], kpe[r, :], add).then_inc(kpe_done, 1)
            split("a", 0, 0)
            split("a", 0, 1)
            dve.wait_ge(c_done, 2)
            normed(1)
            inverse_rms(2)
            dve.wait_ge(stage_hi_done, 1)
            for h in range(2):
                last = low(k_lo[r, h, :], kpe[r, :], k_hi[r, h, :])
            last.then_inc(o2_done, 1)
            split("a", 0, 2)
            split("a", 0, 3)
            dve.wait_ge(c_done, 3)
            normed(2)
            nc.vector.memset(sw[:], 0.0).then_inc(sw_zero, 1)
            dve.wait_ge(tabB_landed, 16)
            dve.wait_ge(lnc_landed, 16)
            dve.wait_ge(sw_zero, 1)
            pairs("a", A_PAIRS, None, "b")
            pairs("b", B_PAIRS, "a", None, "eo")
            columns("eo", KT, (PJ, PJ + 1), "u0")
            ffn(0)
            pads()
            pairs("c", C_PAIRS, None, None, "oo")
            columns("oo", KT, (PJ, PJ + 1), "u1")
            ffn(1)
            norm(6, None)

        @block.gpsimd
        def _(pool):
            tt, sub, mul, add = nc.gpsimd.tensor_tensor, ALU.subtract, ALU.mult, ALU.add

            def columns(nth):
                for m in range(1, 7):
                    pool.wait_ge(square_done, 8 * nth + 7 + m + 1)
                    if m == 1:
                        tt(to[:], squares[0][:], squares[1][:], add).then_inc(acc_done, 1)
                    else:
                        pool.wait_ge(acc_done, 6 * nth + m + 3)
                        tt(to[:], to[:], squares[m % 2][:], add).then_inc(acc_done, 1)

            def norm_low(n):
                name = NORMS[n]
                g0 = END[name] - WIDTH[name]
                for k, (hi, lo) in enumerate(norm_dst(name)):
                    pool.wait_ge(xn_hi_done, g0 + k + 1)
                    tt(lo, p[:, (g0 + k) % 4, :], hi.bitcast(F32), sub).then_inc(xn_done, 1)

            def normalise(kind, pair, t):
                pool.wait_ge(rden_done, tau(kind, pair) + (t + 1))
                n = 2 if kind == "c" else 1
                pu = p[:, t % 4, :].rearrange("p (n w) -> p n w", n=n)
                r = rden[:, n * t:n * t + n].unsqueeze(2).to_broadcast([P, n, S // n])
                tt(pu, pu, r, mul).then_inc(norm_done, 1)

            def biases(pair, h):
                for kind in range(3):
                    last = tt(bt[:, h, kind, :], cm[:, kind, :], wide[:, h, WIDE_OFF[kind]:WIDE_OFF[kind] + BAND], sub)
                last.then_inc(bias_ready, 1)

            def load_biases(pair):
                pool.dma_start(wide, bias[bass.ds((pair - 8) * 2, 2)].rearrange("h p w -> p h w")).then_inc(bias_landed, 16)

            def project(kind, pair, s):
                if kind == "a" and s in (6, 8):
                    h = 0 if s == 6 else 1
                    pool.wait_ge(stage_hi_done, pair * 2 + (h + 2))
                    tt(q_lo[:, h, :], (rq, rk)[h][:], q_hi[:, h, :].bitcast(F32), sub).then_inc(q_lo_done, 1)
                if kind == "a" and s in (2, 3):
                    h = s - 2
                    pool.wait_ge(rope_t_done, pair * 2 + (h + 1))
                    dst = (rq, rk)[h][:]
                    tt(dst, dst, sw[:], add).then_inc(rope_done, 1)
                if kind == "b" and s in (4, 6):
                    m = 0 if s == 4 else 1
                    pool.wait_ge(swap_done, (pair - 4) * 2 + (m + 1))
                    tt(sw[:], sw[:], tB[:, 2 * m + 1, :], mul).then_inc(rope_m_done, 1)
                    pool.wait_ge(rope_m_done, (pair - 4) * 2 + (m + 1))
                    pool.wait_ge(rope_t_done, pair * 2 + (m + 1))
                    dst = (rq, rk)[m][:]
                    tt(dst, dst, sw[:], add).then_inc(rope_done, 1)
                if kind == "c" and s == 0:
                    pool.wait_ge(bias_ready, (pair - 8) * 2)
                    load_biases(pair)
                if kind == "c" and s in (3, 7):
                    h = s // 4
                    pool.wait_ge(bias_landed, (pair - 7) * 16)
                    pool.wait_ge(min_done, tau(kind, pair) + (2 * h - 2))
                    biases(pair, h)

            def work(kind, pair, j):
                t = tile_at(kind, j, GAP[kind])
                if t is not None:
                    normalise(kind, pair, t)
                if j == OUT_SPLIT[kind]:
                    out_low(kind, pair)

            def heads(before, kind, pair, after):
                for s in range(SLOTS):
                    if after == "b":
                        project(after, pair + 1, s)
                    if before:
                        work(before, pair - 1, s + SLOTS)
                    work(kind, pair, s)
                    if s == 0:
                        project(kind, pair, SLOTS)
                    if after and after != "b":
                        project(after, pair + 1, s)

            def out_low(kind, pair):
                pool.wait_ge(o_hi_done, pair + 1)
                k = pair - 8 if kind == "c" else pair
                dst, hi = o_lo[:, bass.ds(k, 1), :], o_hi[:, bass.ds(k, 1), :]
                tt(dst, of[:].rearrange("p (k s) -> p k s", k=1), hi.bitcast(F32), sub).then_inc(o_lo_done, 1)

            def pairs(kind, n, before, after):
                p0 = PAIR0[kind]
                if kind == "c":
                    pool.wait_ge(cmask_landed, 16)
                    pool.wait_ge(bias_landed, 16)
                    biases(p0, 0)
                    biases(p0, 1)
                elif before is None:
                    for s in range(SLOTS):
                        project(kind, p0, s)
                heads(before, kind, p0, kind)
                with pool.Fori(p0 + 1, p0 + n - 1) as pair:
                    heads(kind, kind, pair, kind)
                heads(kind, kind, p0 + n - 1, after)
                if after is None:
                    for j in range(SLOTS, SPAN):
                        work(kind, p0 + n - 1, j)

            def ffn(layer):
                with pool.Fori(0, FT) as f:
                    pool.wait_ge(hid_hi_done, f + (layer * FT + 1))
                    tt(h_lo[:, bass.ds(f, 1), :], rk[:].rearrange("p (k s) -> p k s", k=1),
                       h_hi[:, bass.ds(f, 1), :].bitcast(F32), sub).then_inc(hid_lo_done, 1)

            pool.sem_inc(o_lo_done, CR_OLO)
            for k in range(0, KT, 2):
                pool.wait_ge(square_done, k // 2 + 1)
                pool.wait_ge(square2_done, k // 2 + 1)
                tt(first_squares[k], first_squares[k], first_squares[k + 1][:], add).then_inc(acc_done, 1)
            norm_low(0)
            norm_low(1)
            norm_low(2)
            pool.wait_ge(tabB_landed, 16)
            pairs("a", A_PAIRS, None, "b")
            pairs("b", B_PAIRS, "a", None)
            columns(0)
            pool.dma_start(cm, cmask).then_inc(cmask_landed, 16)
            load_biases(8)
            ffn(0)
            columns(1)
            pairs("c", C_PAIRS, None, None)
            columns(2)
            ffn(1)
            columns(3)


def _rows(w, cols):
    import numpy as np
    a = np.ascontiguousarray(w[:, cols]) if not isinstance(cols, slice) else w[:, cols]
    if a.shape[1] < P:
        a = np.concatenate([a, np.zeros((a.shape[0], P - a.shape[1]), a.dtype)], axis=1)
    return [a[k * P:(k + 1) * P] for k in range(a.shape[0] // P)]


def _chunks(tiles, per):
    import numpy as np
    zero = np.zeros((P, P), np.float32)
    tiles = [zero if t is None else t for t in tiles]
    a = np.stack(tiles).reshape(len(tiles) // per, per, P, P)
    return np.ascontiguousarray(a.transpose(0, 2, 1, 3).reshape(len(tiles) // per, P, per * P))


def _layout(i):
    import numpy as np
    ar = np.arange
    nat = (ar(S) % 8) * 64 + ar(S) // 8
    w_in, q_up, kv_up = i["ev_w_in"][0], i["ev_w_q_up"][0], i["ev_w_kv_up"][0]
    swap = np.r_[16:32, 0:16]
    t = {}
    kpe = QR + KVR + ar(ROPE)
    q0, q1, kv = (_rows(w_in, ar(m * P, m * P + P)) for m in range(3))
    t["a0"] = sum([[q0[k], q1[k]] for k in range(KT)], []) + _rows(w_in, np.r_[kpe, kpe[swap]]) + kv
    t["a"], t["b"] = [], []
    for pr in range(A_PAIRS):
        for h in (2 * pr, 2 * pr + 1):
            c = h * QA
            t["a"] += _rows(q_up, np.r_[c + ar(QA), c + NOPE + swap])
        c0, c1 = 4 * pr * 64, (4 * pr + 2) * 64
        t["a"] += _rows(kv_up, np.r_[c0 + 64 + ar(64), c1 + 64 + ar(64)]) + [None]
        t["a"] += _rows(kv_up, np.r_[c0 + ar(64), c1 + ar(64)]) + [None]
        for m in (1, 0, 2):
            t["b"] += _rows(w_in, 416 + 512 * m + 128 * pr + ar(P))
    t["eo"] = sum([_rows(i["ev_w_out"][0], m * P + ar(P)) for m in range(8)], [])
    t["oo"] = sum([_rows(i["od_w_out"][0], m * P + ar(P)) for m in range(8)], [])
    t["c"] = sum([_rows(i["od_w_qkv"][0], m * DM + pr * P + ar(P)) for pr in range(8) for m in (1, 0, 2)], [])
    for l in range(2):
        t[f"u{l}"] = sum([_rows(i[w][l], f * P + ar(P)) for f in range(FT) for w in ("ffn_w_gate", "ffn_w_up")], [])
        t[f"d{l}"] = sum([_rows(i["ffn_w_down"][l], m * P + ar(P)) + [None, None] for m in range(8)], [])
        t[f"u{l}"][:16] = sum([[t[f"u{l}"][k], t[f"u{l}"][KT + k]] for k in range(KT)], [])
    for name in ("eo", "oo"):
        a, b = t[name][:8], t[name][8:16]
        t[name][:16] = a[:6] + b[:6] + [a[6], b[6], a[7], b[7]]
    arrays = {f"w_{k}": _chunks(v, PER[k]) for k, v in t.items()}
    arrays["xT"] = np.ascontiguousarray(i["x"][0][nat].T.reshape(KT, P, S).transpose(1, 0, 2))
    g = np.zeros((P, 48), np.float32)
    for name, a in (("ev", i["ev_norm"][0]), ("f0", i["ffn_norm"][0]), ("od", i["od_norm"][0]),
                    ("f1", i["ffn_norm"][1]), ("fin", i["final_norm"]), ("q", i["ev_q_norm"][0]),
                    ("kv", i["ev_kv_norm"][0])):
        a = a.reshape(-1, P).T
        g[:, GAIN[name]:GAIN[name] + a.shape[1]] = a
    arrays["gains"] = g
    arrays["consts"] = np.stack([np.eye(P, dtype=np.float32), np.ones((P, P), np.float32)], axis=1)

    def rope(dim):
        inv = np.float32(10000.0) ** (-np.arange(0, dim, 2, dtype=np.float32) / np.float32(dim))
        ang = nat.astype(np.float32)[None, :] * inv.astype(np.float32)[:, None]
        return np.cos(ang), np.sin(ang)

    ca, sa = rope(ROPE)
    cb, sbn = rope(HD)
    scale = float(QA) ** -0.5
    a = np.zeros((P, 2, S), np.float32)
    a[0:NOPE, 0] = -scale
    a[NOPE:QA, 0] = -scale * np.r_[ca, ca]
    a[QA:, 0] = np.r_[-sa, sa]
    a[0:ROPE, 1] = np.r_[ca, ca]
    a[NOPE:QA, 1] = -scale * np.r_[-sa, sa]
    arrays["tabA"] = a
    C, R = np.tile(np.r_[cb, cb], (2, 1)), np.tile(np.r_[-sbn, sbn], (2, 1))
    arrays["tabB"] = np.ascontiguousarray(np.stack([C, R, -0.125 * C, -0.125 * R], axis=1).astype(np.float32))
    d = np.abs(nat[:, None] - nat[None, :])
    count = sum(((d % dil == 0) & (d // dil <= win // (2 * dil))).astype(np.float32)
                for win, dil in ((128, 1), (512, 4), (2048, 16)))
    lnc = np.where(count > 0, -np.log(np.maximum(count, 1)), 1e30).astype(np.float32)
    arrays["lnc"] = np.ascontiguousarray(lnc.reshape(4, P, S).transpose(1, 0, 2))
    cm = np.zeros((P, 3, BAND), np.float32)
    for kind, j in enumerate((0, 1, 3)):
        qc = 16 * j + np.arange(P) // 8
        kc = BAND_START[j] // 8 + np.arange(BAND) // 8
        start = np.clip(qc - 8, 0, 48)[:, None]
        cm[:, kind] = np.where((kc[None] >= start) & (kc[None] < start + 16), 0.0, 1e30)
    arrays["cmask"] = cm
    rpb = i["od_rpb"][0]
    pad = np.zeros((16, 15, 31 + 17 + 17), np.float32)
    pad[:, :, 17:48] = rpb
    wide = np.zeros((16, P, 48, 8), np.float32)
    for q in range(P):
        qc, r = q // 8, q % 8
        wide[:, q] = pad[:, 7 - r:15 - r, 16 - qc:64 - qc].transpose(0, 2, 1)
    arrays["bias"] = wide.reshape(16, P, WIDE)
    return arrays, nat


def kernel(**inputs):
    import numpy as np
    import concourse.bacc as bacc
    from concourse.bass_utils import run_bass_kernel_spmd

    arrays, nat = _layout({k: np.asarray(v) for k, v in inputs.items()})
    nc = bacc.Bacc("TRN2", target_bir_lowering=False, num_devices=1)
    ap = {k: nc.dram_tensor(f"in_{k}", v.shape, mybir.dt.from_np(v.dtype), kind="ExternalInput").ap()
          for k, v in arrays.items()}
    out = nc.dram_tensor("out_y", (P, KT, S), F32, kind="ExternalOutput").ap()
    build(nc, ap["xT"], ap["gains"], ap["consts"], ap["tabA"], ap["tabB"], ap["lnc"], ap["cmask"], ap["bias"],
          {k: ap[f"w_{k}"] for k in STREAM}, out)
    r = run_bass_kernel_spmd(nc, [{f"in_{k}": v for k, v in arrays.items()}], core_ids=[0])
    y = r.results[0]["out_y"].transpose(1, 0, 2).reshape(DM, S).T
    back = np.empty_like(y)
    back[nat] = y
    return back[None]
```
